# Optimizing a Trainium2 kernel written in Bass

```python
import math
import jax, jax.numpy as jnp
from jax import lax
import numpy as np

D_MODEL = 1024
BATCH = 1
SEQ = 256
DEPTH = 1

N_META = 16
HG_HEADS = 4
HG_HEAD_DIM = 128
D_HG = HG_HEADS * HG_HEAD_DIM
HG_CHUNK = 64
D_LRU = D_MODEL
LRU_BLOCKS = 8
LRU_BLOCK = D_LRU // LRU_BLOCKS
CONV_WIDTH = 4
LRU_C = 8.0
N_GROUPS = 4
EXPERTS_PER_GROUP = 8
N_EXPERTS = N_GROUPS * EXPERTS_PER_GROUP
TOP_K = 2
D_EXPERT = 512
MOE_BLOCK = 512
EPS = 1e-6
SPLIT_SIZES = (D_HG, D_HG, D_HG, D_HG, D_LRU, D_LRU, D_MODEL, D_MODEL)
D_IN = sum(SPLIT_SIZES)


def rmsnorm(x, g):
    xf = x.astype(jnp.float32)
    y = xf * lax.rsqrt(jnp.mean(xf * xf, axis=-1, keepdims=True) + EPS)
    return (y * g.astype(jnp.float32)).astype(x.dtype)

def hgrn2_chunked(q, k, v, log_f):
    B, T, H, DK = q.shape
    DV = v.shape[-1]
    C = HG_CHUNK
    NC = T // C

    def to_chunks(a):
        return a.reshape(B, NC, C, H, a.shape[-1]).transpose(1, 0, 3, 2, 4)

    qc, kc, vc, gc = to_chunks(q), to_chunks(k), to_chunks(v), to_chunks(log_f)
    causal = jnp.tril(jnp.ones((C, C), dtype=bool))[:, :, None]

    def step(S, inp):
        qb, kb, vb, gb = inp
        G = jnp.cumsum(gb, axis=2)
        diff = G[:, :, :, None, :] - G[:, :, None, :, :]
        decay = jnp.exp(jnp.where(causal, diff, -jnp.inf))
        scores = jnp.einsum('bhtd,bhsd,bhtsd->bhts', qb, kb, decay)
        o = (jnp.einsum('bhts,bhsv->bhtv', scores, vb)
             + jnp.einsum('bhtd,bhdv->bhtv', qb * jnp.exp(G), S))
        G_end = G[:, :, -1:, :]
        S_new = (jnp.exp(G_end[:, :, 0, :])[..., None] * S
                 + jnp.einsum('bhsd,bhsv->bhdv', kb * jnp.exp(G_end - G), vb))
        return S_new, o

    S0 = jnp.zeros((B, H, DK, DV), jnp.float32)
    _, o = lax.scan(step, S0, (qc, kc, vc, gc))
    return o.transpose(1, 0, 3, 2, 4).reshape(B, T, H, DV)

def hgrn2_branch(q_pre, f_pre, i_pre, og_pre, lb, norm_g):
    B, T, _ = q_pre.shape
    f32 = jnp.float32
    lb = lb.astype(f32)
    fp = f_pre.astype(f32)
    f = lb + (1.0 - lb) * jax.nn.sigmoid(fp)
    log_f = jnp.log(f)
    k = (1.0 - lb) * jax.nn.sigmoid(-fp)
    pad = (-N_META) % HG_CHUNK

    def prep(a):
        a = jnp.pad(a.astype(f32), ((0, 0), (pad, 0), (0, 0)))
        return a.reshape(B, T + pad, HG_HEADS, HG_HEAD_DIM)

    o = hgrn2_chunked(prep(q_pre), prep(k), prep(i_pre), prep(log_f))[:, pad:]
    o = o * lax.rsqrt(jnp.mean(o * o, axis=-1, keepdims=True) + EPS)
    o = o * norm_g.astype(f32).reshape(HG_HEADS, HG_HEAD_DIM)
    o = o.reshape(B, T, D_HG) * jax.nn.sigmoid(og_pre.astype(f32))
    return o.astype(q_pre.dtype)

def rglru_branch(xb, yb, conv_w, conv_b, w_r, b_r, w_i, b_i, lam):
    B, T, _ = xb.shape
    f32 = jnp.float32
    xc = lax.conv_general_dilated(
        xb, conv_w[:, None, :].astype(xb.dtype), window_strides=(1,),
        padding=[(CONV_WIDTH - 1, 0)], dimension_numbers=('NWC', 'WIO', 'NWC'),
        feature_group_count=D_LRU) + conv_b.astype(xb.dtype)
    xh = xc.reshape(B, T, LRU_BLOCKS, LRU_BLOCK)
    r = jax.nn.sigmoid(jnp.einsum('btni,nij->btnj', xh, w_r).reshape(B, T, D_LRU).astype(f32)
                       + b_r.astype(f32))
    i = jax.nn.sigmoid(jnp.einsum('btni,nij->btnj', xh, w_i).reshape(B, T, D_LRU).astype(f32)
                       + b_i.astype(f32))
    log_a = -LRU_C * r * jax.nn.softplus(-lam.astype(f32))
    a = jnp.exp(log_a)
    u = jnp.sqrt(-jnp.expm1(2.0 * log_a)) * (i * xc.astype(f32))

    def combine(left, right):
        a_l, b_l = left
        a_r, b_r2 = right
        return a_l * a_r, a_r * b_l + b_r2

    _, h = lax.associative_scan(combine, (a, u), axis=1)
    return (h * jax.nn.gelu(yb.astype(f32))).astype(xb.dtype)

def hier_moe(h, w_group, b_group, w_router, b_router, w_gate, w_up, w_down):
    B, T, D = h.shape
    N = B * T
    f32 = jnp.float32
    hf = h.reshape(N, D)
    group_logits = (hf @ w_group).astype(f32) + b_group.astype(f32)
    p_group = jax.nn.softmax(group_logits, axis=-1)
    g_sel = jnp.argmax(group_logits, axis=-1).astype(jnp.int32)
    p_sel = jnp.take_along_axis(p_group, g_sel[:, None], axis=-1)
    exp_logits = jnp.einsum('nd,gde->nge', hf, w_router).astype(f32) + b_router.astype(f32)
    sel_logits = jnp.take_along_axis(exp_logits, g_sel[:, None, None], axis=1)[:, 0]
    top_vals, top_idx = lax.top_k(sel_logits, TOP_K)
    weights = p_sel * jax.nn.softmax(top_vals, axis=-1)
    expert_ids = g_sel[:, None] * EXPERTS_PER_GROUP + top_idx.astype(jnp.int32)

    A = N * TOP_K
    e_flat = expert_ids.reshape(A)
    w_flat = weights.reshape(A)
    tok_flat = jnp.arange(A, dtype=jnp.int32) // TOP_K
    order = jnp.argsort(e_flat)
    e_sorted = e_flat[order]
    counts = jnp.zeros((N_EXPERTS,), jnp.int32).at[e_flat].add(1)
    starts = jnp.cumsum(counts) - counts
    pcounts = (counts + MOE_BLOCK - 1) // MOE_BLOCK * MOE_BLOCK
    pends = jnp.cumsum(pcounts)
    pstarts = pends - pcounts
    dest = pstarts[e_sorted] + (jnp.arange(A, dtype=jnp.int32) - starts[e_sorted])
    n_blocks = -(-A // MOE_BLOCK) + N_EXPERTS
    n_slots = n_blocks * MOE_BLOCK
    slot_tok = jnp.zeros((n_slots,), jnp.int32).at[dest].set(tok_flat[order])
    slot_w = jnp.zeros((n_slots,), f32).at[dest].set(w_flat[order])
    block_start = jnp.arange(n_blocks, dtype=jnp.int32) * MOE_BLOCK
    block_expert = jnp.minimum(jnp.searchsorted(pends, block_start, side='right'),
                               N_EXPERTS - 1).astype(jnp.int32)

    def run_block(args):
        toks, wts, e = args
        xb = hf[toks]
        y = (jax.nn.silu(xb @ w_gate[e]) * (xb @ w_up[e])) @ w_down[e]
        return y * wts[:, None].astype(y.dtype)

    ys = lax.map(run_block, (slot_tok.reshape(n_blocks, MOE_BLOCK),
                             slot_w.reshape(n_blocks, MOE_BLOCK), block_expert))
    out = jnp.zeros((N, D), h.dtype).at[slot_tok].add(ys.reshape(n_slots, D).astype(h.dtype))
    return out.reshape(B, T, D)

def mixer(hn, w_in, lb, hg_norm_g, conv_w, conv_b, w_r, b_r, w_i, b_i, lam, w_up_a, w_up_b, w_out):
    proj = hn @ w_in
    idx = [int(c) for c in np.cumsum(SPLIT_SIZES)[:-1]]
    q_pre, f_pre, i_pre, og_pre, lx, ly, ga, gb = jnp.split(proj, idx, axis=-1)
    o_a = hgrn2_branch(q_pre, f_pre, i_pre, og_pre, lb, hg_norm_g)
    o_b = rglru_branch(lx, ly, conv_w, conv_b, w_r, b_r, w_i, b_i, lam)
    merged = jax.nn.sigmoid(ga) * (o_a @ w_up_a) + jax.nn.sigmoid(gb) * (o_b @ w_up_b)
    return merged @ w_out

def first_inputs(seed: int = 0) -> dict:
    key = jax.random.key(seed)
    ks = jax.random.split(key, 26)
    f32 = jnp.float32
    nrm = lambda k, shape, scale: jax.random.normal(k, shape, f32) * scale
    u = jax.random.uniform(ks[13], (DEPTH, D_LRU), f32, minval=0.9, maxval=0.999)
    a0 = u ** (1.0 / LRU_C)
    return {
        "x": nrm(ks[0], (BATCH, SEQ, D_MODEL), 1.0),
        "meta_tokens": nrm(ks[1], (N_META, D_MODEL), 1.0),
        "norm1_g": 1.0 + nrm(ks[2], (DEPTH, D_MODEL), 0.02),
        "w_in": nrm(ks[3], (DEPTH, D_MODEL, D_IN), D_MODEL ** -0.5),
        "hg_lower_bounds": nrm(ks[4], (DEPTH + 1, D_HG), 0.1),
        "hg_norm_g": 1.0 + nrm(ks[5], (DEPTH, D_HG), 0.02),
        "conv_w": nrm(ks[6], (DEPTH, CONV_WIDTH, D_LRU), CONV_WIDTH ** -0.5),
        "conv_b": nrm(ks[7], (DEPTH, D_LRU), 0.01),
        "lru_w_r": nrm(ks[8], (DEPTH, LRU_BLOCKS, LRU_BLOCK, LRU_BLOCK), LRU_BLOCK ** -0.5),
        "lru_b_r": nrm(ks[9], (DEPTH, D_LRU), 0.01),
        "lru_w_i": nrm(ks[10], (DEPTH, LRU_BLOCKS, LRU_BLOCK, LRU_BLOCK), LRU_BLOCK ** -0.5),
        "lru_b_i": nrm(ks[11], (DEPTH, D_LRU), 0.01),
        "lru_lambda": jnp.log(a0) - jnp.log1p(-a0),
        "w_up_a": nrm(ks[14], (DEPTH, D_HG, D_MODEL), D_HG ** -0.5),
        "w_up_b": nrm(ks[15], (DEPTH, D_LRU, D_MODEL), D_LRU ** -0.5),
        "w_out": nrm(ks[16], (DEPTH, D_MODEL, D_MODEL), D_MODEL ** -0.5),
        "norm2_g": 1.0 + nrm(ks[17], (DEPTH, D_MODEL), 0.02),
        "w_group": nrm(ks[18], (DEPTH, D_MODEL, N_GROUPS), D_MODEL ** -0.5),
        "b_group": nrm(ks[19], (DEPTH, N_GROUPS), 0.01),
        "w_router": nrm(ks[20], (DEPTH, N_GROUPS, D_MODEL, EXPERTS_PER_GROUP), D_MODEL ** -0.5),
        "b_router": nrm(ks[21], (DEPTH, N_GROUPS, EXPERTS_PER_GROUP), 0.01),
        "w_gate": nrm(ks[22], (DEPTH, N_EXPERTS, D_MODEL, D_EXPERT), D_MODEL ** -0.5),
        "w_up": nrm(ks[23], (DEPTH, N_EXPERTS, D_MODEL, D_EXPERT), D_MODEL ** -0.5),
        "w_down": nrm(ks[24], (DEPTH, N_EXPERTS, D_EXPERT, D_MODEL), D_EXPERT ** -0.5),
        "final_g": 1.0 + nrm(ks[25], (D_MODEL,), 0.02),
    }

def first_block(x, meta_tokens, norm1_g, w_in, hg_lower_bounds, hg_norm_g, conv_w, conv_b,
              lru_w_r, lru_b_r, lru_w_i, lru_b_i, lru_lambda, w_up_a, w_up_b, w_out,
              norm2_g, w_group, b_group, w_router, b_router, w_gate, w_up, w_down, final_g):
    B = x.shape[0]
    meta = jnp.broadcast_to(meta_tokens[None].astype(x.dtype), (B, N_META, D_MODEL))
    h = jnp.concatenate([meta, x], axis=1)
    lbs = jnp.cumsum(jax.nn.softmax(hg_lower_bounds.astype(jnp.float32), axis=0), axis=0)
    for l in range(DEPTH):
        mix = mixer(rmsnorm(h, norm1_g[l]), w_in[l], lbs[l], hg_norm_g[l], conv_w[l], conv_b[l],
                    lru_w_r[l], lru_b_r[l], lru_w_i[l], lru_b_i[l], lru_lambda[l],
                    w_up_a[l], w_up_b[l], w_out[l])
        h = h + mix.astype(h.dtype)
        ffn = hier_moe(rmsnorm(h, norm2_g[l]), w_group[l], b_group[l], w_router[l], b_router[l],
                       w_gate[l], w_up[l], w_down[l])
        h = h + ffn.astype(h.dtype)
    return rmsnorm(h, final_g)[:, N_META:]


HEAD_DIM = 64
ATTN_HEADS_PER_GROUP = 8
DILATED_GROUPS = ((128, 1), (512, 4), (2048, 16))
N_DIL = len(DILATED_GROUPS)
ATTN_WIDTH = ATTN_HEADS_PER_GROUP * HEAD_DIM
ROPE_DIM = HEAD_DIM // 4
ROPE_THETA = 500000.0
BLK = 128
SGU_CHUNK = 128
SGU_GROUPS = 8
SGU_WIDTH = D_MODEL // 2
SGU_GROUP_DIM = SGU_WIDTH // SGU_GROUPS
D_FF = -(-8 * D_MODEL // (3 * 256)) * 256
QKV_COLS = 3 * N_DIL * ATTN_WIDTH
IN_COLS = QKV_COLS + 2 * SGU_WIDTH + 2 * D_MODEL


def rmsnorm_2(x, g):
    xf = x.astype(jnp.float32)
    y = xf * lax.rsqrt(jnp.mean(xf * xf, axis=-1, keepdims=True) + EPS)
    return (y * g.astype(jnp.float32)).astype(x.dtype)

def layernorm(x, g, b):
    xf = x.astype(jnp.float32)
    mu = jnp.mean(xf, axis=-1, keepdims=True)
    xc = xf - mu
    y = xc * lax.rsqrt(jnp.mean(xc * xc, axis=-1, keepdims=True) + EPS)
    return (y * g.astype(jnp.float32) + b.astype(jnp.float32)).astype(x.dtype)

def partial_rope(t, positions):
    half = ROPE_DIM // 2
    inv_freq = ROPE_THETA ** (-jnp.arange(0, ROPE_DIM, 2, dtype=jnp.float32) / ROPE_DIM)
    ang = positions.astype(jnp.float32)[..., None] * inv_freq
    cos = jnp.cos(ang)[:, :, None, :]
    sin = jnp.sin(ang)[:, :, None, :]
    tf = t.astype(jnp.float32)
    x1, x2 = tf[..., :half], tf[..., half:ROPE_DIM]
    rot = jnp.concatenate([x1 * cos - x2 * sin, x2 * cos + x1 * sin, tf[..., ROPE_DIM:]], axis=-1)
    return rot.astype(t.dtype)

def dilated_attention(q, k, v, window, dilation):
    B, S, H, Dh = q.shape
    span = window // dilation
    L = -(-S // dilation)
    L_pad = -(-L // BLK) * BLK
    S_pad = L_pad * dilation
    nb = L_pad // BLK
    pad = ((0, 0), (0, S_pad - S), (0, 0), (0, 0))

    def strided(t):
        t = jnp.pad(t, pad).reshape(B, L_pad, dilation, H, Dh).transpose(0, 2, 1, 3, 4)
        return t.reshape(B, dilation, nb, BLK, H, Dh)

    def with_prev(t):
        prev = jnp.pad(t, ((0, 0), (0, 0), (1, 0), (0, 0), (0, 0), (0, 0)))[:, :, :-1]
        return jnp.concatenate([prev, t], axis=3)

    qs = strided(q * (Dh ** -0.5))
    kb = with_prev(strided(k))
    vb = with_prev(strided(v))
    s = jnp.einsum('brnqhd,brnkhd->brnhqk', qs, kb, preferred_element_type=jnp.float32)

    i = jnp.arange(BLK)[:, None]
    j = jnp.arange(2 * BLK)[None, :]
    diff = BLK + i - j
    band = (diff >= 0) & (diff <= span)
    key_exists = (jnp.arange(nb)[:, None, None] > 0) | (j >= BLK)[None]
    mask = band[None] & key_exists
    s = jnp.where(mask[None, None, :, None], s, -jnp.inf)

    m = jnp.max(s, axis=-1, keepdims=True)
    p = jnp.exp(s - m)
    den = jnp.sum(p, axis=-1)
    lse = m[..., 0] + jnp.log(den)
    o = jnp.einsum('brnhqk,brnkhd->brnqhd', p, vb.astype(jnp.float32))
    o = o / jnp.swapaxes(den, -1, -2)[..., None]

    o = o.reshape(B, dilation, L_pad, H, Dh).transpose(0, 2, 1, 3, 4).reshape(B, S_pad, H, Dh)[:, :S]
    lse = jnp.swapaxes(lse, -1, -2).reshape(B, dilation, L_pad, H).transpose(0, 2, 1, 3)
    lse = lse.reshape(B, S_pad, H)[:, :S]
    return o.astype(q.dtype), lse

def spatial_gating(uv, ln_g, ln_b, w_s, b_s):
    B, S, _ = uv.shape
    z = jax.nn.gelu(uv, approximate=False)
    u, v = z[..., :SGU_WIDTH], z[..., SGU_WIDTH:]
    v = layernorm(v, ln_g, ln_b)
    vc = v.reshape(B, S // SGU_CHUNK, SGU_CHUNK, SGU_GROUPS, SGU_GROUP_DIM)
    causal = jnp.tril(jnp.ones((SGU_CHUNK, SGU_CHUNK), dtype=bool))
    w_causal = jnp.where(causal[None], w_s, jnp.zeros_like(w_s))
    mixed = jnp.einsum('gts,bnsgc->bntgc', w_causal, vc)
    mixed = mixed + jnp.transpose(b_s)[None, None, :, :, None]
    return u * mixed.reshape(B, S, SGU_WIDTH)

def second_inputs(seed: int = 0) -> dict:
    key = jax.random.key(seed)
    ks = jax.random.split(key, 18)
    f32 = jnp.float32
    x = jax.random.normal(ks[0], (BATCH, SEQ, D_MODEL), f32)
    offset = jax.random.randint(ks[1], (BATCH, 1), 0, 4096, dtype=jnp.int32)
    positions = offset + jnp.arange(SEQ, dtype=jnp.int32)[None, :]
    nrm = lambda k, shape, fan_in: jax.random.normal(k, shape, f32) * (fan_in ** -0.5)
    return {
        "x": x,
        "positions": positions,
        "norm1_g": 1.0 + 0.02 * jax.random.normal(ks[2], (DEPTH, D_MODEL), f32),
        "w_in": nrm(ks[3], (DEPTH, D_MODEL, IN_COLS), D_MODEL),
        "sgu_ln_g": 1.0 + 0.02 * jax.random.normal(ks[4], (DEPTH, SGU_WIDTH), f32),
        "sgu_ln_b": 0.02 * jax.random.normal(ks[5], (DEPTH, SGU_WIDTH), f32),
        "w_spatial": nrm(ks[6], (DEPTH, SGU_GROUPS, SGU_CHUNK, SGU_CHUNK), SGU_CHUNK),
        "b_spatial": 1.0 + 0.1 * jax.random.normal(ks[7], (DEPTH, SGU_GROUPS, SGU_CHUNK), f32),
        "w_proj_attn": nrm(ks[8], (DEPTH, ATTN_WIDTH, D_MODEL), ATTN_WIDTH),
        "w_proj_sgu": nrm(ks[9], (DEPTH, SGU_WIDTH, D_MODEL), SGU_WIDTH),
        "w_out": nrm(ks[10], (DEPTH, D_MODEL, D_MODEL), D_MODEL),
        "norm2_g": 1.0 + 0.02 * jax.random.normal(ks[11], (DEPTH, D_MODEL), f32),
        "w_ffn_gate": nrm(ks[12], (DEPTH, D_MODEL, D_FF), D_MODEL),
        "w_ffn_up": nrm(ks[13], (DEPTH, D_MODEL, D_FF), D_MODEL),
        "w_ffn_down": nrm(ks[14], (DEPTH, D_FF, D_MODEL), D_FF),
        "final_g": 1.0 + 0.02 * jax.random.normal(ks[15], (D_MODEL,), f32),
    }

def second_block(x, positions, norm1_g, w_in, sgu_ln_g, sgu_ln_b, w_spatial, b_spatial,
              w_proj_attn, w_proj_sgu, w_out, norm2_g, w_ffn_gate, w_ffn_up, w_ffn_down,
              final_g):
    B, S, _ = x.shape
    for l in range(DEPTH):
        h = rmsnorm_2(x, norm1_g[l])
        proj = h @ w_in[l]
        qkv = proj[..., :QKV_COLS].reshape(B, S, 3, N_DIL, ATTN_HEADS_PER_GROUP, HEAD_DIM)
        uv = proj[..., QKV_COLS:QKV_COLS + 2 * SGU_WIDTH]
        gate_a = jax.nn.sigmoid(proj[..., QKV_COLS + 2 * SGU_WIDTH:QKV_COLS + 2 * SGU_WIDTH + D_MODEL])
        gate_b = jax.nn.sigmoid(proj[..., QKV_COLS + 2 * SGU_WIDTH + D_MODEL:])

        outs, lses = [], []
        for g, (window, dilation) in enumerate(DILATED_GROUPS):
            q = partial_rope(qkv[:, :, 0, g], positions)
            k = partial_rope(qkv[:, :, 1, g], positions)
            o, lse = dilated_attention(q, k, qkv[:, :, 2, g], window, dilation)
            outs.append(o)
            lses.append(lse)
        alpha = jax.nn.softmax(jnp.stack(lses, axis=0), axis=0)
        attn = jnp.sum(alpha[..., None].astype(x.dtype) * jnp.stack(outs, axis=0), axis=0)
        attn = attn.reshape(B, S, ATTN_WIDTH)

        sgu = spatial_gating(uv, sgu_ln_g[l], sgu_ln_b[l], w_spatial[l], b_spatial[l])

        merged = gate_a * (attn @ w_proj_attn[l]) + gate_b * (sgu @ w_proj_sgu[l])
        x = x + merged @ w_out[l]

        h2 = rmsnorm_2(x, norm2_g[l])
        ff = jax.nn.silu(h2 @ w_ffn_gate[l]) * (h2 @ w_ffn_up[l])
        x = x + ff @ w_ffn_down[l]
    return rmsnorm_2(x, final_g)


def setup_inputs(seed=0):
    out = dict(first_inputs(seed))
    for name, value in second_inputs(seed + 1).items():
        if name != "x":
            out[name + "_2"] = value
    return out


def reference(
    x, meta_tokens, norm1_g, w_in, hg_lower_bounds, hg_norm_g, conv_w, conv_b, lru_w_r, lru_b_r,
    lru_w_i, lru_b_i, lru_lambda, w_up_a, w_up_b, w_out, norm2_g, w_group, b_group, w_router,
    b_router, w_gate, w_up, w_down, final_g, positions_2, norm1_g_2, w_in_2, sgu_ln_g_2,
    sgu_ln_b_2, w_spatial_2, b_spatial_2, w_proj_attn_2, w_proj_sgu_2, w_out_2, norm2_g_2,
    w_ffn_gate_2, w_ffn_up_2, w_ffn_down_2, final_g_2,
):
    x = first_block(
        x, meta_tokens, norm1_g, w_in, hg_lower_bounds, hg_norm_g, conv_w, conv_b, lru_w_r,
        lru_b_r, lru_w_i, lru_b_i, lru_lambda, w_up_a, w_up_b, w_out, norm2_g, w_group, b_group,
        w_router, b_router, w_gate, w_up, w_down, final_g,
    )
    return second_block(
        x, positions_2, norm1_g_2, w_in_2, sgu_ln_g_2, sgu_ln_b_2, w_spatial_2, b_spatial_2,
        w_proj_attn_2, w_proj_sgu_2, w_out_2, norm2_g_2, w_ffn_gate_2, w_ffn_up_2, w_ffn_down_2,
        final_g_2,
    )


_drawn_inputs = setup_inputs


def setup_inputs(seed=0):
    import zlib

    import numpy as np

    out = dict(_drawn_inputs(seed))
    spreads = {}
    factors = {'hg_norm_g': 2.843,
     'lru_b_r': 8.0,
     'lru_b_i': 8.0,
     'b_group': 2.949,
     'b_router': 3.994,
     'norm1_g_2': 4.861,
     'sgu_ln_g_2': 8.0,
     'sgu_ln_b_2': 8.0,
     'norm2_g_2': 10.885,
     'final_g_2': 8.282}
    for name, (base, spread) in spreads.items():
        noise = np.random.default_rng([zlib.crc32(name.encode()), seed]).standard_normal(out[name].shape)
        drawn = base * np.exp(spread * noise) if base else spread * noise
        out[name] = __import__('jax').numpy.asarray(drawn.astype(out[name].dtype))
    for name, factor in factors.items():
        out[name] = (out[name] * factor).astype(out[name].dtype)
    return out
```

```python
from contextlib import ExitStack

import numpy as np
import concourse.bass as bass
from concourse import mybir

ALU = mybir.AluOpType
ACT = mybir.ActivationFunctionType
F32 = mybir.dt.float32
I32 = mybir.dt.int32
AX_X = mybir.AxisListType.X

P = 128
D = 1024
KC = D // P
T = 256
NT = T // P
META = 16
TT = META + T
EPS = 1e-6
HEADS = 4
NE = 32
GROUPS = 4
EPG = NE // GROUPS
CAP = 64
PAIRS = NE // 2
PASSES = T // CAP
SLOTS = NE * CAP
DE = 512
FF = 2816
FC = FF // P
RING = 6
UW = 4096
AH = 8
NG = 3
HD = 64
SG = 8
NEG = -1.0e30
INV_FREQ = [float(np.float32(500000.0 ** (-j / 16.0))) for j in range(0, 16, 2)]
LEVELS = [64, 32, 16, 8, 4, 2, 1]

VEC_ROWS = [("norm1_g", 8), ("hg_lower_bounds", 8), ("hg_norm_g", 4), ("conv_w", 32), ("conv_b", 8),
            ("lru_b_r", 8), ("lru_b_i", 8), ("lru_lambda", 8), ("norm1_g_2", 8), ("norm2_g_2", 8),
            ("b_spatial_2", 8)]
VEC_AT = {}
NVR = 0
for _name, _n in VEC_ROWS:
    VEC_AT[_name] = NVR
    NVR += _n

B1_UNITS = ["i", "f", "q", "lx0", "lx1", "ly0", "ly1", "og", "ga0", "ga1", "lru", "gb0", "gb1",
            "up_a", "up_b0", "up_b1", "out0", "out1"]
MOE_UNITS = ["g0", "g1", "u0", "u1", "d0", "d1"]
B2_UNITS = (["q0", "q1", "q2", "k0", "k1", "k2", "v0", "v1", "v2", "uv0", "uv1", "ga0", "ga1", "gb0", "gb1",
             "pa", "ps", "out0", "out1"] + [f"ff{n}" for n in range(11)] + [f"fd{n}" for n in range(6)])
MOE0 = len(B1_UNITS)
B2_0 = MOE0 + 6 * PAIRS
assert MOE0 % RING == 0
B1_OUTS = 47
W1_COL = {"q": 0, "f": 512, "i": 1024, "og": 1536, "lx0": 2048, "lx1": 2560, "ly0": 3072, "ly1": 3584,
          "ga0": 4096, "ga1": 4608, "gb0": 5120, "gb1": 5632}


STATS = {"n1": 0, "n2": 3, "f1": 5, "n3": 7, "ln": 9, "n4": 11, "f2": 13}
ROWS = {"n1": 0, "n2": 3, "n3": 5, "n4": 7}


def transfers(name, block):
    return 2 if (name == "lru" or (block == 2 and name.startswith("ff"))) else 1


def landed_values():
    total = [0] * RING
    value = {}
    for u in range(B2_0 + len(B2_UNITS)):
        if u < MOE0:
            n = transfers(B1_UNITS[u], 1)
        elif u < B2_0:
            n = 1
        else:
            n = transfers(B2_UNITS[u - B2_0], 2)
        total[u % RING] += 16 * n
        value[u] = total[u % RING]
    return value


LANDED = landed_values()


def used(u):
    if u < MOE0:
        name = B1_UNITS[u]
        if name == "lru":
            return "lru_products", 2 * KC
        if name.startswith("up"):
            return ("up_a", 1) if name == "up_a" else ("up_b", KC)
        if name.startswith("out"):
            return "out_merged", u - B1_UNITS.index("out0") + 1
        return "projected", 3 + 4 * (u if u < 10 else u - 1)
    if u < B2_0:
        j = (u - MOE0) % 6
        assert u >= B2_0 - 6
        return ("gates", "ups", "y_ready")[j // 2], PAIRS
    n = u - B2_0
    if n < 11:
        return "projected", B1_OUTS + 2 * (n + 1)
    if n < 15:
        return "projected", B1_OUTS + 22 + 4 * (n - 10)
    if n < 17:
        return ("proj_a", 1) if n == 15 else ("proj_b", KC)
    if n < 19:
        return "out_merged2", n - 16
    if n < 30:
        return "ff", 2 * (n - 18)
    return "out_ff_cols", n - 29


def build(nc, A, out):
    ctx = ExitStack()
    with ctx:
        def sb(name, shape, dt=F32):
            return ctx.enter_context(nc.sbuf_tensor(name, shape, dt))

        sems = {}

        def S(name):
            if name not in sems:
                sems[name] = ctx.enter_context(nc.semaphore(name))
            return sems[name]

        bank = [ctx.enter_context(nc.psum_tensor(f"bank{b}", [P, 512], F32)) for b in range(8)]
        ring = sb("ring", [P, RING, UW])
        ident = sb("ident", [P, P])
        ones = sb("ones", [P, P])
        h = sb("h", [P, NT, D])
        vec = sb("vec", [P, NVR])
        cst = sb("cst", [P, 64])
        stat = sb("stat", [P, 128])
        route = sb("route", [P, 1400])
        idx = sb("idx", [P, 64], I32)
        arena_words = 24552
        arena = sb("arena", [P, arena_words])
        top = {}

        def at(region, words):
            o = top[region]
            top[region] = o + words
            assert o + words <= arena_words, (region, o + words)
            return arena[:, o:o + words]

        hf_d = nc.dram_tensor("hf_rows", [T, D], F32).ap()
        y_d = nc.dram_tensor("expert_rows", [PASSES * SLOTS, D], F32).ap()
        list_d = nc.dram_tensor("token_list", [PASSES * SLOTS, 1], I32).ap()

        top["m1"] = 0
        wz = at("m1", 3072)
        xn = wz.rearrange("p (t d) -> p t d", t=3)
        hnT = at("m1", KC * TT).rearrange("p (c t) -> p c t", c=KC)
        v1 = at("m1", 1536).rearrange("p (t d) -> p t d", t=3)
        fkg0 = top["m1"]
        sf = at("m1", HEADS * TT).rearrange("p (c t) -> p c t", c=HEADS)
        kk = at("m1", HEADS * TT).rearrange("p (c t) -> p c t", c=HEADS)
        kx = at("m1", HEADS * T).rearrange("p (c t) -> p c t", c=HEADS)
        Gx = at("m1", HEADS * T).rearrange("p (c t) -> p c t", c=HEADS)
        Gm = at("m1", HEADS * META).rearrange("p (c t) -> p c t", c=HEADS)
        lx = at("m1", KC * (3 + TT)).rearrange("p (c t) -> p c t", c=KC)
        ly = at("m1", KC * T).rearrange("p (c t) -> p c t", c=KC)
        og = at("m1", HEADS * T).rearrange("p (c t) -> p c t", c=HEADS)
        ga = at("m1", KC * T).rearrange("p (c t) -> p c t", c=KC)
        zo = top["m1"]
        qx = at("m1", HEADS * T).rearrange("p (c t) -> p c t", c=HEADS)
        z1 = at("m1", HEADS * T)
        PT = at("m1", 1024).rearrange("p (c t) -> p c t", c=8)
        St = at("m1", 1024).rearrange("p (k h v) -> p k h v", k=2, h=HEADS)
        kT = z1.rearrange("p (k n) -> p k n", k=2)
        meta = z1
        maskw = at("m1", 8 * P).bitcast(I32).rearrange("p (l t) -> p l t", l=8)
        oT = at("m1", HEADS * T).rearrange("p (c t) -> p c t", c=HEADS)
        m1_end = top["m1"]
        vecrows = oT.rearrange("p c t -> p (c t)")[:, 0:P]
        W = [wz[:, 0:1024], wz[:, 1024:2048]]
        z = [wz[:, 2048:3072], z1]
        kE = wz[:, 2048:3072]
        top["xc"] = fkg0
        xc = at("xc", KC * TT).rearrange("p (c t) -> p c t", c=KC)
        assert top["xc"] <= fkg0 + 2 * HEADS * TT
        lrur = lx[:, :, 0:TT]
        o0 = 0
        lrui = arena[:, o0:o0 + KC * TT].rearrange("p (c t) -> p c t", c=KC)
        lrua = arena[:, zo:zo + KC * TT].rearrange("p (c t) -> p c t", c=KC)
        lrut = arena[:, zo + KC * TT:zo + 2 * KC * TT].rearrange("p (c t) -> p c t", c=KC)
        assert zo + 2 * KC * TT <= m1_end - HEADS * T
        rsn = v1[:, 0:2, :].rearrange("p t d -> p (t d)")
        gb = arena[:, fkg0 + 2 * HEADS * TT:fkg0 + 2 * HEADS * TT + KC * T].rearrange("p (c t) -> p c t", c=KC)
        mT = hnT[:, :, 0:T]

        top["moe"] = 0
        hf = at("moe", NT * D).rearrange("p (t d) -> p t d", t=NT)
        hfT = at("moe", KC * T).rearrange("p (c t) -> p c t", c=KC)
        g2b = at("moe", D)
        fgb = at("moe", D)
        rw = at("moe", KC * 36).rearrange("p (c e) -> p c e", c=KC)
        xg = at("moe", D)
        xgT = at("moe", KC * 2 * CAP).rearrange("p (c t) -> p c t", c=KC)
        sg = at("moe", DE)
        hid = at("moe", DE)
        hT = at("moe", 4 * 2 * CAP).rearrange("p (k n) -> p k n", k=4)
        ysb = at("moe", D)
        yg = at("moe", 4 * D).rearrange("p (k d) -> p k d", k=4)
        zeros_i = at("moe", PASSES * SLOTS // P).bitcast(I32)

        top["b2"] = 0
        xn2 = at("b2", NT * D).rearrange("p (t d) -> p t d", t=NT)
        hn2 = at("b2", KC * T).rearrange("p (c t) -> p c t", c=KC)
        top["x2"] = 0
        qk = [xn2[:, :, 0:512], xn2[:, :, 512:1024]]
        qkT = at("b2", 24 * T).rearrange("p (c t) -> p c t", c=24)
        vv = at("b2", NT * NG * 512).rearrange("p (t d) -> p t d", t=NT)
        uv = at("b2", NT * D).rearrange("p (t d) -> p t d", t=NT)
        gate = at("b2", 2 * KC * T).rearrange("p (c t) -> p c t", c=2 * KC)
        amask = at("b2", 1152)
        ffo = top["b2"]
        scw = at("b2", 1536)
        sc = [scw[:, 0:768], scw[:, 768:1536]]
        attn = at("b2", NT * 512).rearrange("p (t d) -> p t d", t=NT)
        rtmp = scw[:, 1024:1536].rearrange("p (k n) -> p k n", k=4)
        wsT = xn2[:, 0, :].rearrange("p (g t) -> p g t", g=SG)
        lngb = xn2[:, 1, :]
        PTb = at("b2", 768)
        aT = xn2[:, 0, :].rearrange("p (c t) -> p c t", c=4)
        sT = xn2[:, 1, :].rearrange("p (c t) -> p c t", c=4)
        wsr = attn.rearrange("p t d -> p (t d)")
        mT2 = hn2
        ffT = qkT.rearrange("p c t -> p (c t)")[:, 0:FC * T].rearrange("p (c t) -> p c t", c=FC)
        sgf = scw[:, 0:1024].rearrange("p (k t) -> p k t", k=4)
        fgb2 = gate.rearrange("p c t -> p (c t)")[:, 0:D]
        outr = gate.rearrange("p c t -> p (c t)")[:, D:3 * D].rearrange("p (t d) -> p t d", t=NT)

        def not_zero(eng, name, value):
            if not (isinstance(value, int) and value == 0):
                eng.wait_ge(S(name), value)

        def V(name, k=0, n=1):
            return vec[:, VEC_AT[name] + k:VEC_AT[name] + k + n]

        def bc(ap, shape, axis):
            return ap.unsqueeze(axis).to_broadcast(shape)

        negh = cst[:, 0:1]
        lbv = cst[:, 4:8]
        omlb = cst[:, 8:12]
        sp8 = cst[:, 12:20]
        tmp8 = cst[:, 20:28]
        m2sp = cst[:, 28:36]
        egA = cst[:, 36:40]
        pdt = cst[:, 40:48]

        def w3(u, k):
            return ring[:, u % RING, :].rearrange("p (k n) -> p k n", k=k)

        bias36 = route[:, 0:36]
        lg = route[:, 40:112].rearrange("p (t e) -> p t e", t=2)
        iota32 = route[:, 112:144]
        base_l = route[:, 144:176]
        base_s = route[:, 176:208]
        tokid = route[:, 208:210]
        ustr = route[:, 210:338]
        rt = route[:, 340:1400]
        block = ctx.enter_context(nc.Block())

        @block.sync
        def _(sp):
            w1 = A["w_in"][0].rearrange("(k p) n -> p k n", p=P)
            w2 = A["w_in_2"][0].rearrange("(k p) n -> p k n", p=P)

            def slot_free(u):
                if u >= RING:
                    name, value = used(u - RING)
                    sp.wait_ge(S(name), value)

            def load(u, src, dst=None):
                dst = ring[:, u % RING, :] if dst is None else dst
                sp.dma_start(dst, src).then_inc(S(f"landed{u % RING}"), 16)

            sp.wait_ge(S("params_issued"), 1)
            for u, name in enumerate(B1_UNITS):
                slot_free(u)
                if name in W1_COL:
                    load(u, w1[:, :, W1_COL[name]:W1_COL[name] + 512], w3(u, KC))
                elif name == "lru":
                    load(u, A["lru_w_r"][0].rearrange("n i j -> i n j"), w3(u, 32)[:, 0:8, :])
                    load(u, A["lru_w_i"][0].rearrange("n i j -> i n j"), w3(u, 32)[:, 8:16, :])
                elif name == "up_a":
                    load(u, A["w_up_a"][0].rearrange("(k p) n -> p k n", p=P), w3(u, 4))
                else:
                    src = A["w_up_b"] if name.startswith("up_b") else A["w_out"]
                    load(u, src[0].rearrange("(k p) n -> p k n", p=P)[:, 4 * int(name[-1]):4 * int(name[-1]) + 4, :],
                         w3(u, 4))

            gate_w = A["w_gate"][0].rearrange("e (k p) n -> e p k n", p=P)
            up_w = A["w_up"][0].rearrange("e (k p) n -> e p k n", p=P)
            down_w = A["w_down"][0].rearrange("e (k p) n -> e p k n", p=P)

            def expert_unit(j, e2):
                src = {"g": gate_w, "u": up_w, "d": down_w}[MOE_UNITS[j][0]]
                return src[bass.ds(e2 + int(MOE_UNITS[j][1]), 1)].rearrange("e p k n -> p e k n")

            def expert_dst(j):
                return w3(j, KC if MOE_UNITS[j][0] != "d" else 4).unsqueeze(1)

            for j in range(6):
                slot_free(MOE0 + j)
                sp.dma_start(expert_dst(j), expert_unit(j, 0)).then_inc(S(f"landed{j}"), 16)
            with sp.Fori(1, PAIRS) as i:
                for j in range(6):
                    sp.wait_ge(S(("gates", "ups", "y_ready")[j // 2]), i)
                    sp.dma_start(expert_dst(j), expert_unit(j, 2 * i)).then_inc(S(f"landed{j}"), 16)

            sp.wait_ge(S("flag_set"), 1)
            over = sp.value_load(idx[0:1, 40:41], min_val=0, max_val=T)
            with sp.If(over > CAP):
                sp.wait_ge(S("y_ready"), PAIRS)
                with sp.Fori(0, PASSES - 1) as a:
                    with sp.Fori(0, PAIRS) as i:
                        for j in range(6):
                            sp.wait_ge(S("over_y"), PAIRS * a + i + 1)
                            sp.dma_start(expert_dst(j), expert_unit(j, 2 * i)).then_inc(S("over_landed"), 16)
                sp.wait_ge(S("over_y"), (PASSES - 1) * PAIRS + 1)

            for n, name in enumerate(B2_UNITS):
                u = B2_0 + n
                slot_free(u)
                if n < 15:
                    load(u, w2[:, :, 512 * n:512 * n + 512], w3(u, KC))
                elif name in ("pa", "ps"):
                    src = A["w_proj_attn_2"] if name == "pa" else A["w_proj_sgu_2"]
                    load(u, src[0].rearrange("(k p) n -> p k n", p=P), w3(u, 4))
                elif name.startswith("out"):
                    c = 4 * int(name[-1])
                    load(u, A["w_out_2"][0].rearrange("(k p) n -> p k n", p=P)[:, c:c + 4, :], w3(u, 4))
                elif name.startswith("ff"):
                    c = 256 * int(name[2:])
                    for q, key in enumerate(("w_ffn_gate_2", "w_ffn_up_2")):
                        load(u, A[key][0].rearrange("(k p) n -> p k n", p=P)[:, :, c:c + 256],
                             w3(u, 2 * KC)[:, KC * q:KC * q + KC, :])
                else:
                    c = 4 * int(name[2:])
                    m = min(4, FC - c)
                    load(u, A["w_ffn_down_2"][0].rearrange("(k p) n -> p k n", p=P)[:, c:c + m, :],
                         w3(u, 4)[:, 0:m, :])
            for t in range(NT):
                sp.wait_ge(S("out_rows"), t + 1)
                sp.dma_start(out[0, t * P:(t + 1) * P, :], outr[:, t, :]).then_inc(S("stored"), 16)
            sp.wait_ge(S("stored"), 16 * NT)

        @block.gpsimd
        def _(pool):
            n_link = [0]

            def link(ins):
                n_link[0] += 1
                ins.then_inc(S("pool_chain"), 1)
                pool.wait_ge(S("pool_chain"), n_link[0])

            link(pool.memset(ident[:, :], 0.0))
            link(pool.memset(ones[:, :], 1.0))
            link(pool.affine_select(out=ident[:, :], in_=ident[:, :], compare_op=ALU.not_equal, fill=1.0,
                                    base=0, pattern=[[-1, P]], channel_multiplier=1))
            link(pool.memset(negh, -0.5))
            link(pool.memset(lx[:, :, 0:3], 0.0))
            pool.iota(idx[:, 60:61], [[0, 1]], base=0, channel_multiplier=1).then_inc(S("iotas"), 1)
            pool.iota(maskw[:, 7, :], [[1, P]], base=0, channel_multiplier=0).then_inc(S("iotas"), 1)

            def power(name, n, count, parts, scale):
                pool.wait_ge(S("norm_sums"), STATS[name] + count)
                link(pool.tensor_scalar(stat[0:parts, n + 8:n + 9], stat[0:parts, n:n + 1], scale, EPS,
                                        ALU.mult, ALU.add))
                pool.tensor_tensor(stat[0:parts, n + 16:n + 17], stat[0:parts, n + 8:n + 9],
                                   negh[0:parts, :], ALU.pow).then_inc(S("norm_rstd"), 1)

            for j, (parts, tile) in enumerate(((META, 2), (P, 0), (P, 1))):
                power("n1", tile, j + 1, parts, 1.0 / D)

            link(pool.memset(ustr, 1.0))
            link(pool.affine_select(out=ustr, in_=ustr, compare_op=ALU.is_gt, fill=0.0,
                                    base=0, pattern=[[1, P]], channel_multiplier=-1))
            pool.iota(iota32, [[1, 32]], base=0, channel_multiplier=0,
                      allow_small_or_imprecise_dtypes=True).then_inc(S("route_consts"), 1)
            pool.iota(base_l, [[1, PAIRS], [PAIRS * CAP, 2]], base=0, channel_multiplier=0,
                      allow_small_or_imprecise_dtypes=True).then_inc(S("route_consts"), 1)
            pool.iota(base_s, [[CAP, 32]], base=0, channel_multiplier=0,
                      allow_small_or_imprecise_dtypes=True).then_inc(S("route_consts"), 1)
            pool.iota(idx[:, 50:52], [[P, 2]], base=0, channel_multiplier=1).then_inc(S("route_consts"), 1)

            for t in range(NT):
                power("n2", 24 + t, t + 1, P, 1.0 / D)

            pool.wait_ge(S("out_merged"), 2)
            link(pool.memset(zeros_i, 0))
            pool.dma_start(list_d.rearrange("(p n) a -> p (n a)", p=P), zeros_i).then_inc(S("list_zeroed"), 16)
            pool.wait_ge(S("list_zeroed"), 16)
            pool.wait_ge(S("slots_set"), 4)
            for j in range(4):
                pool.indirect_dma_start(list_d, bass.IndirectOffsetOnAxis(ap=idx[:, j:j + 1], axis=0),
                                        idx[:, 50 + j // 2:51 + j // 2], None).then_inc(S("list_put"), 16)
            pool.wait_ge(S("list_put"), 64)
            pool.dma_start(idx[:, 16:32], list_d[0:SLOTS].rearrange("(p n) a -> p (n a)", p=P)) \
                .then_inc(S("list_back"), 16)
            pool.wait_ge(S("list_back"), 16)
            pool.wait_ge(S("hf_stored"), 32)

            def gather(dst, src, column):
                return pool.indirect_dma_start(dst, None, src,
                                               bass.IndirectOffsetOnAxis(ap=column, axis=0))

            gather(xg[:, :], hf_d, idx[:, 16:17]).then_inc(S("rows_in"), 16)
            for i in range(1, PAIRS):
                pool.wait_ge(S("rows_turned"), i)
                gather(xg[:, :], hf_d, idx[:, 16 + i:17 + i]).then_inc(S("rows_in"), 16)
            pool.wait_ge(S("y_stored"), 16 * PAIRS)

            pool.wait_ge(S("flag_set"), 1)
            over = pool.value_load(idx[0:1, 40:41], min_val=0, max_val=T)
            with pool.If(over > CAP):
                pool.wait_ge(S("rows_turned"), PAIRS)
                with pool.Fori(0, PASSES - 1) as a:
                    pool.dma_start(idx[:, 16:32], list_d[bass.ds((a + 1) * SLOTS, SLOTS)]
                                   .rearrange("(p n) a -> p (n a)", p=P)).then_inc(S("over_list"), 16)
                    pool.wait_ge(S("over_list"), 16 * a + 16)
                    pool.sem_inc(S("over_go"), 1)
                    for i in range(PAIRS):
                        gather(xg[:, :], hf_d, idx[:, 16 + i:17 + i]).then_inc(S("over_rows"), 16)
                        pool.wait_ge(S("over_stored"), 16 * PAIRS * a + 16 * (i + 1))
                        pool.sem_inc(S("over_go"), 1)
                for j in range(4):
                    gather(yg[:, j, :], y_d, idx[:, 4 + j:5 + j]).then_inc(S("y_back"), 16)
            with pool.If(over < CAP + 1):
                for j in range(4):
                    gather(yg[:, j, :], y_d[0:SLOTS], idx[:, 4 + j:5 + j]).then_inc(S("y_back"), 16)

            for t in range(NT):
                power("f1", 48 + t, t + 1, P, 1.0 / D)
            for t in range(NT):
                power("n3", 50 + t, t + 1, P, 1.0 / D)

            def keep(view, base, pattern, cm, op):
                link(pool.affine_select(out=view, in_=view, compare_op=op, fill=NEG, base=base,
                                        pattern=pattern, channel_multiplier=cm))

            pool.wait_ge(S("x2_ready"), NT)
            link(pool.memset(amask, 0.0))
            for g, dil in enumerate((1, 4, 16)):
                for tile, o, n in ((1, T * g, T), (0, NG * T + P * g, P)):
                    view = amask[:, o:o + n]
                    keep(view, P * tile, [[-1, n]], 1, ALU.is_ge)
                    if g == 0:
                        keep(view, P - P * tile, [[1, n]], -1, ALU.is_ge)
            pool.iota(scw[:, 0:T].bitcast(I32), [[-1, T]], base=P + 0, channel_multiplier=1) \
                .then_inc(S("diff_iota"), 1)
            pool.wait_ge(S("ws_loaded"), 16)
            ws3 = wsr.rearrange("p (g s) -> p g s", g=SG)
            pool.affine_select(out=ws3, in_=ws3, compare_op=ALU.is_ge, fill=0.0, base=0,
                               pattern=[[0, SG], [-1, P]], channel_multiplier=1).then_inc(S("ws_masked"), 1)

            for t in range(NT):
                power("ln", 56 + t, t + 1, P, 1.0)
            for t in range(NT):
                power("n4", 64 + 0 + t, t + 1, P, 1.0 / D)
            for t in range(NT):
                power("f2", 88 + t, t + 1, P, 1.0 / D)

        @block.tensor
        def _(pe):
            mm = nc.tensor.matmul
            tr = nc.tensor.transpose

            def take(u):
                pe.wait_ge(S(f"landed{u % RING}"), LANDED[u])

            def turn_rows(rows, name, src, n_tiles):
                for j in range(n_tiles):
                    tile, n = rows[j]
                    pe.wait_ge(S("norm_rows"), ROWS[name] + j + 1)
                    for half in range(2):
                        for c in range(4):
                            k = 4 * half + c
                            last = tr(bank[2 * j + half][:, c * n:(c + 1) * n], src[0:n, tile, k * P:(k + 1) * P],
                                      ident[0:n, 0:n])
                        last.then_inc(S("norm_turned"), 1)

            pe.wait_ge(S("pool_chain"), 3)
            pe.wait_ge(S("vec_loaded"), 16 * len(VEC_ROWS))
            tr(bank[7][:, 0:NVR], vecrows[0:NVR, :], ident[0:NVR, 0:NVR]).then_inc(S("vec_turned"), 1)
            turn_rows(((2, META), (0, P), (1, P)), "n1", xn, 3)

            n_out = [0]

            def out_bank():
                n = n_out[0]
                n_out[0] += 1
                if n >= 4:
                    pe.wait_ge(S("evac"), n - 3)
                return bank[n % 4]

            def project_cols(u, first, hn, lo, n):
                take(u)
                for m in range(4):
                    b = out_bank()
                    for k in range(KC):
                        last = mm(b[:, 0:n], w3(u, KC)[:, k, m * P:(m + 1) * P], hn[:, k, lo:lo + n],
                                  start=(k == 0), stop=(k == KC - 1))
                    last.then_inc(S("projected"), 1)

            def project_rows(u, tiles, hn):
                take(u)
                for lo, n in tiles:
                    b = out_bank()
                    for k in range(KC):
                        last = mm(b[0:n, :], hn[:, k, lo:lo + n], w3(u, KC)[:, k, :],
                                  start=(k == 0), stop=(k == KC - 1))
                    last.then_inc(S("projected"), 1)

            pe.wait_ge(S("norm_done"), 2 * ROWS["n1"] + 6)
            project_rows(0, ((0, META), (META, P), (META + P, P)), hnT)
            project_cols(1, 0, hnT, 0, TT)
            project_cols(2, 0, hnT, META, T)
            project_cols(3, 0, hnT, 0, TT)

            for part in range(2):
                n = (META, P)[part]
                pe.wait_ge(S("k_end"), part + 1)
                for hd in range(HEADS):
                    last = tr(bank[4][0:n, hd * P:(hd + 1) * P],
                              kE[:, hd * P:hd * P + n], ident[:, :])
                last.then_inc(S("k_turned"), 1)
                pe.wait_ge(S("kT_ready"), part + 1)
                for hd in range(HEADS):
                    last = mm(bank[5][:, hd * P:(hd + 1) * P], kT[0:n, part, hd * P:(hd + 1) * P],
                              v1[0:n, (2, 0)[part], hd * P:(hd + 1) * P], start=True, stop=True)
                last.then_inc(S("kv"), 1)
                if part == 0:
                    pe.wait_ge(S("state"), 1)
            pe.wait_ge(S("state"), 2)

            def level(l):
                if l < 7:
                    pe.wait_ge(S("z_ready"), l + 1)
                if l >= 2:
                    pe.wait_ge(S("picked"), l - 1)
                for c in range(8):
                    lo = (c // 2) * T + (c % 2) * P
                    if l < 7:
                        a = b = z[l % 2][:, lo:lo + P]
                    else:
                        a = kx.rearrange("p c t -> p (c t)")[:, lo:lo + P]
                        b = qx.rearrange("p c t -> p (c t)")[:, lo:lo + P]
                    last = mm(bank[4 + 2 * (l % 2) + c // 4][:, (c % 4) * P:(c % 4 + 1) * P], a, b,
                              start=True, stop=True)
                last.then_inc(S("levels"), 1)

            project_cols(4, 0, hnT, 0, TT)
            level(0)
            level(1)
            project_cols(5, 0, hnT, META, T)
            level(2)
            level(3)
            project_cols(6, 0, hnT, META, T)
            level(4)
            level(5)
            project_cols(7, 0, hnT, META, T)
            level(6)
            level(7)
            project_cols(8, 0, hnT, META, T)
            pe.wait_ge(S("picked"), 8)
            pe.wait_ge(S("qe_ready"), 1)
            for hd in range(HEADS):
                for c in range(2):
                    o = bank[4 + hd // 2][:, (hd % 2) * T + c * P:(hd % 2) * T + (c + 1) * P]
                    mm(o, v1[:, c, hd * P:(hd + 1) * P], PT[:, 2 * hd + c, :], start=True, stop=False)
                    last = mm(o, St[:, c, hd, :], qx[:, hd, c * P:(c + 1) * P], start=False, stop=True)
            last.then_inc(S("o_ready"), 1)
            project_cols(9, 0, hnT, META, T)
            pe.wait_ge(S("o_squared"), 2)
            for c in range(2):
                last = mm(bank[6 + c][:, :], ones[:, :], W[0][:, c * 512:(c + 1) * 512], start=True, stop=True)
            last.then_inc(S("o_sums"), 1)
            take(10)
            pe.wait_ge(S("o_mean"), 1)
            for b in range(KC):
                for q in range(2):
                    n = 2 * b + q
                    if b == 0:
                        pe.wait_ge(S("conv"), KC)
                    if n >= 4:
                        pe.wait_ge(S("lru_gates"), n - 3)
                    last = mm(bank[4 + n % 4][:, 0:TT], w3(10, 32)[:, 8 * q + b, :], xc[:, b, :],
                              start=True, stop=True)
                    last.then_inc(S("lru_products"), 1)
            project_cols(11, 0, hnT, META, T)
            project_cols(12, 0, hnT, META, T)
            pe.wait_ge(S("evac"), n_out[0])
            pe.wait_ge(S("oa_ready"), 1)
            take(13)
            for m in range(KC):
                for k in range(HEADS):
                    last = mm(bank[m // 2][:, (m % 2) * T:(m % 2 + 1) * T], w3(13, 4)[:, k, m * P:(m + 1) * P],
                              oT[:, k, :], start=(k == 0), stop=(k == HEADS - 1))
            last.then_inc(S("up_a"), 1)
            pe.wait_ge(S("lru_gates"), 16)
            pe.wait_ge(S("ob_ready"), 1)
            take(14)
            take(15)
            for m in range(KC):
                for k in range(KC):
                    last = mm(bank[4 + m // 2][:, (m % 2) * T:(m % 2 + 1) * T],
                              w3(14 + k // 4, 4)[:, k % 4, m * P:(m + 1) * P],
                              ly[:, k, :], start=(k == 0), stop=(k == KC - 1))
                last.then_inc(S("up_b"), 1)

            def out_projection(u0, src, ready, n_units, total):
                for k in range(total):
                    if k % 4 == 0:
                        take(u0 + k // 4)
                    if k == 0:
                        pe.wait_ge(S(ready), total if total == KC else FC)
                    for b in range(4):
                        last = mm(bank[b][:, :], src[:, k, (b // 2) * P:(b // 2 + 1) * P],
                                  w3(u0 + k // 4, 4)[:, k % 4, (b % 2) * 512:(b % 2 + 1) * 512],
                                  start=(k == 0), stop=(k == total - 1))
                    if k % 4 == 3 or k == total - 1:
                        last.then_inc(S("out_" + ready), 1)

            out_projection(16, mT, "merged", 2, KC)

            pe.wait_ge(S("h_added"), 2)
            turn_rows(((0, P), (1, P)), "n2", hf, 2)
            pe.wait_ge(S("norm_done"), 2 * ROWS["n2"] + 4)
            pe.wait_ge(S("rw_loaded"), 16 * 5)
            for t in range(NT):
                for k in range(KC):
                    last = mm(bank[4 + t][:, 0:36], hfT[:, k, t * P:(t + 1) * P], rw[:, k, :],
                              start=(k == 0), stop=(k == KC - 1))
                last.then_inc(S("logits"), 1)
            pe.wait_ge(S("chosen"), 1)
            M = rt[:, 0:64]
            mm(bank[6][:, 0:32], ustr, M[:, 0:32], start=True, stop=True)
            mm(bank[6][:, 32:64], ones[:, :], M[:, 0:32], start=True, stop=False)
            mm(bank[6][:, 32:64], ustr, M[:, 32:64], start=False, stop=True)
            mm(bank[6][:, 64:96], ones[:, :], M[:, 0:32], start=True, stop=False)
            mm(bank[6][:, 64:96], ones[:, :], M[:, 32:64], start=False, stop=True).then_inc(S("places"), 1)

            def turn_pair():
                for k in range(KC):
                    last = tr(bank[2 + k // 4][:, (k % 4) * 2 * CAP:(k % 4 + 1) * 2 * CAP],
                              xg[:, k * P:(k + 1) * P], ident[:, :])
                return last

            def products(b, units):
                for k in range(KC):
                    for e in range(2):
                        last = mm(bank[b][e * CAP:(e + 1) * CAP, :], xgT[:, k, e * CAP:(e + 1) * CAP],
                                  w3(units[e], KC)[:, k, :], start=(k == 0), stop=(k == KC - 1))
                return last

            def turn_hidden():
                for k in range(4):
                    last = tr(bank[6][:, k * P:(k + 1) * P], hid[:, k * P:(k + 1) * P], ident[:, :])
                return last

            def down():
                for k in range(4):
                    for half in range(2):
                        for e in range(2):
                            last = mm(bank[4 + half][e * CAP:(e + 1) * CAP, :], hT[:, k, e * CAP:(e + 1) * CAP],
                                      w3(4 + e, 4)[:, k, half * 512:(half + 1) * 512],
                                      start=(k == 0), stop=(k == 3))
                return last

            base = [LANDED[MOE0 + j] for j in range(6)]

            def pair(i, last_pair):
                for j in range(2):
                    pe.wait_ge(S(f"landed{j}"), 16 * i + base[j])
                pe.wait_ge(S("turned_copied"), 2 * i + 2)
                products(0, (0, 1)).then_inc(S("gates"), 1)
                for j in range(2, 4):
                    pe.wait_ge(S(f"landed{j}"), 16 * i + base[j])
                products(1, (2, 3)).then_inc(S("ups"), 1)
                if not last_pair:
                    pe.wait_ge(S("rows_in"), 16 * i + 32)
                    turn_pair().then_inc(S("rows_turned"), 1)
                pe.wait_ge(S("hidden"), i + 1)
                turn_hidden().then_inc(S("hid_turned"), 1)
                for j in range(4, 6):
                    pe.wait_ge(S(f"landed{j}"), 16 * i + base[j])
                pe.wait_ge(S("hT_ready"), i + 1)
                not_zero(pe, "y_copied", 2 * i)
                down().then_inc(S("y_ready"), 1)

            pe.wait_ge(S("rows_in"), 16)
            turn_pair().then_inc(S("rows_turned"), 1)
            pair(0, False)
            with pe.Fori(1, PAIRS - 1) as i:
                pair(i, False)
            pair(PAIRS - 1, True)

            pe.wait_ge(S("flag_set"), 1)
            over = pe.value_load(idx[0:1, 40:41], min_val=0, max_val=T)
            with pe.If(over > CAP):
                pe.sem_inc(S("over_y"), 1)
                with pe.Fori(0, (PASSES - 1) * PAIRS) as n:
                    pe.wait_ge(S("over_rows"), 16 * n + 16)
                    turn_pair().then_inc(S("over_turned"), 1)
                    pe.wait_ge(S("over_xgT"), n + 1)
                    pe.wait_ge(S("over_landed"), 96 * n + 96)
                    products(0, (0, 1))
                    products(1, (2, 3)).then_inc(S("over_gate_up"), 1)
                    pe.wait_ge(S("over_hidden"), n + 1)
                    turn_hidden().then_inc(S("over_hid"), 1)
                    pe.wait_ge(S("over_hT"), n + 1)
                    down().then_inc(S("over_y"), 1)

            turn_rows(((0, P), (1, P)), "n3", xn2, 2)
            pe.wait_ge(S("norm_done"), 2 * ROWS["n3"] + 4)
            tiles = ((0, P), (P, P))

            def turn_qk(n):
                pe.wait_ge(S("roped"), n + 1)
                for t in range(NT):
                    m = 2 * n + t
                    if m >= 4:
                        pe.wait_ge(S("qk_copied"), m - 3)
                    for c in range(4):
                        last = tr(bank[4 + m % 4][:, c * P:(c + 1) * P], qk[n % 2][:, t, c * P:(c + 1) * P],
                                  ident[:, :])
                    last.then_inc(S("qk_turned"), 1)

            for n in range(11):
                project_rows(B2_0 + n, tiles, hn2)
                if 1 <= n <= 6:
                    turn_qk(n - 1)

            pe.wait_ge(S("ws_masked"), 1)
            pe.wait_ge(S("qk_copied"), 12)
            for g in range(SG):
                last = tr(bank[4 + g // 4][:, (g % 4) * P:(g % 4 + 1) * P], wsr[:, g * P:(g + 1) * P], ident[:, :])
            last.then_inc(S("ws_turned"), 1)

            n_feat = [0]

            def gate_chunk():
                n = n_feat[0]
                u = B2_0 + 11 + n // 4
                if n % 4 == 0:
                    take(u)
                pe.wait_ge(S("evac"), n_out[0] - (1 if n >= 2 else 0))
                b = bank[n % 2]
                for k in range(KC):
                    last = mm(b[:, 0:T], w3(u, KC)[:, k, (n % 4) * P:(n % 4 + 1) * P], hn2[:, k, :],
                              start=(k == 0), stop=(k == KC - 1))
                last.then_inc(S("projected"), 1)
                n_feat[0] += 1
                n_out[0] += 1

            def scores(n):
                hd, tile = n // 2, 1 - n % 2
                keys = T if tile else P
                lo = (hd % 2) * HD
                if n >= 2:
                    pe.wait_ge(S("attn_rows"), n - 1)
                for g in range(NG):
                    c = g * 4 + hd // 2
                    col = g * keys
                    last = mm(bank[4 + 2 * (n % 2) + col // 512][:, col % 512:col % 512 + keys],
                              qkT[lo:lo + HD, c, tile * P:(tile + 1) * P], qkT[lo:lo + HD, 12 + c, 0:keys],
                              start=True, stop=True)
                last.then_inc(S("scores"), 1)

            pe.wait_ge(S("ws_ready"), 2)
            scores(0)
            for n in range(2 * AH):
                hd, tile = n // 2, 1 - n % 2
                nb = NG * (2 if tile else 1)
                gate_chunk()
                pe.wait_ge(S("probs"), n + 1)
                for b in range(nb):
                    last = tr(bank[2 + b // 4][:, (b % 4) * P:(b % 4 + 1) * P],
                              sc[n % 2][:, b * P:(b + 1) * P], ident[:, :])
                last.then_inc(S("probs_turned"), 1)
                if n + 1 < 2 * AH:
                    scores(n + 1)
                pe.wait_ge(S("PT_ready"), n + 1)
                for b in range(nb):
                    g, kt = (b // 2, b % 2) if tile else (b, 0)
                    last = mm(bank[4 + 2 * (n % 2)][:, 0:HD], PTb[:, b * P:(b + 1) * P],
                              vv[:, kt, g * 512 + hd * HD:g * 512 + (hd + 1) * HD],
                              start=(b == 0), stop=(b == nb - 1))
                last.then_inc(S("pv"), 1)
            pe.wait_ge(S("attn_rows"), 2 * AH)
            pe.wait_ge(S("ln_rows"), 2)
            for t in range(NT):
                for g in range(SG):
                    last = mm(bank[4 + t][:, g * HD:(g + 1) * HD], wsT[:, g, :],
                              uv[:, t, 512 + g * HD:512 + (g + 1) * HD], start=True, stop=True)
                last.then_inc(S("mixed"), 1)
            for t in range(NT):
                for c in range(4):
                    last = tr(bank[6 + t][:, c * P:(c + 1) * P], attn[:, t, c * P:(c + 1) * P], ident[:, :])
                last.then_inc(S("attn_turned"), 1)
            pe.wait_ge(S("evac"), n_out[0])
            pe.wait_ge(S("aT_ready"), 2)
            ua = B2_0 + 15
            for q, (src, lo) in enumerate(((aT, 0), (sT, 4))):
                if q == 1:
                    pe.wait_ge(S("sgu_rows"), 2)
                    for t in range(NT):
                        for c in range(4):
                            last = tr(bank[6 + t][:, c * P:(c + 1) * P], uv[:, t, c * P:(c + 1) * P], ident[:, :])
                        last.then_inc(S("sgu_turned"), 1)
                    pe.wait_ge(S("sT_ready"), 2)
                take(ua + q)
                for m in range(KC):
                    for k in range(4):
                        last = mm(bank[lo + m // 2][:, (m % 2) * T:(m % 2 + 1) * T],
                                  w3(ua + q, 4)[:, k, m * P:(m + 1) * P], src[:, k, :],
                                  start=(k == 0), stop=(k == 3))
                    if q == 1:
                        last.then_inc(S("proj_b"), 1)
                if q == 0:
                    last.then_inc(S("proj_a"), 1)
            out_projection(ua + 2, mT2, "merged2", 2, KC)

            pe.wait_ge(S("x3_added"), 2)
            turn_rows(((0, P), (1, P)), "n4", xn2, 2)
            pe.wait_ge(S("norm_done"), 2 * ROWS["n4"] + 4)
            uf = ua + 4
            for c in range(FC):
                u = uf + c // 2
                if c % 2 == 0:
                    take(u)
                if c >= 4:
                    pe.wait_ge(S("ff_cols"), c - 3)
                b = bank[4 + c % 4]
                for q in range(2):
                    for k in range(KC):
                        last = mm(b[:, q * T:(q + 1) * T],
                                  w3(u, 2 * KC)[:, KC * q + k, (c % 2) * P:(c % 2 + 1) * P], hn2[:, k, :],
                                  start=(k == 0), stop=(k == KC - 1))
                last.then_inc(S("ff"), 1)
            out_projection(uf + 11, ffT, "ff_cols", 6, FC)

        @block.scalar
        def _(act):
            A_ = nc.scalar.activation

            def rows(name):
                a = A[name]
                while len(a.shape) > 2:
                    a = a[0] if a.shape[0] == 1 else a.rearrange("a b c -> (a b) c")
                n = 1
                for d in a.shape:
                    n *= d
                if len(a.shape) == 2:
                    return a.rearrange("a (b c) -> (a b) c", c=P)
                return a.rearrange("(b c) -> b c", c=P)

            act.dma_start(meta[0:META, :], A["meta_tokens"]).then_inc(S("x_in0"), 16)
            for t in range(NT):
                act.dma_start(h[:, t, :], A["x"][0, t * P:(t + 1) * P, :]).then_inc(S(f"x_in{t + 1}"), 16)
            for name, n in VEC_ROWS:
                o = VEC_AT[name]
                act.dma_start(vecrows[o:o + n, :], rows(name)).then_inc(S("vec_loaded"), 16)
            act.dma_start(bias36[:, 0:4], A["b_group"].partition_broadcast(P).rearrange("p a b -> p (a b)")).then_inc(S("bias_loaded"), 16)
            act.dma_start(bias36[:, 4:36], A["b_router"].rearrange("a b c -> a (b c)").partition_broadcast(P)
                          .rearrange("p a b -> p (a b)")).then_inc(S("bias_loaded"), 16)
            act.dma_start(idx[:, 56:58], A["positions_2"][0].rearrange("(t p) -> p t", p=P), allow_slow_non_contiguous=True) \
                .then_inc(S("pos_loaded"), 16)
            act.sem_inc(S("params_issued"), 1)

            def squares(name, order, src, junk, col):
                for tile, n, ready in order:
                    act.wait_ge(S(ready[0]), ready[1])
                    A_(junk[0:n, tile, :], src[0:n, tile, :] if tile < NT else meta[0:n, :], ACT.Square,
                       accum_out=stat[0:n, col + tile:col + tile + 1]).then_inc(S("norm_sums"), 1)

            squares("n1", ((2, META, ("x_in0", 16)), (0, P, ("x_in1", 16)), (1, P, ("x_in2", 16))), h, xn, 0)

            n_out = [0]

            def evac(dst, func, parts=P, n=512, extra=None, b=None):
                k = n_out[0]
                n_out[0] += 1
                act.wait_ge(S("projected"), k + 1)
                src = bank[k % 4 if b is None else b][0:parts, 0:n]
                if extra is not None:
                    extra(src)
                A_(dst, src, func).then_inc(S("evac"), 1)

            act.wait_ge(S("lb_diff"), 1)
            A_(lbv, lbv, ACT.Exp).then_inc(S("lb_exp"), 1)
            act.wait_ge(S("lam_abs"), 1)
            A_(m2sp, m2sp, ACT.Exp).then_inc(S("lam_exp"), 1)
            act.wait_ge(S("lam_exp"), 1)
            A_(m2sp, m2sp, ACT.Ln, bias=1.0).then_inc(S("sp_log"), 1)
            for tile, n in ((2, META), (0, P), (1, P)):
                evac(v1[0:n, tile, :], ACT.Copy, n)
            for c in range(4):
                evac(sf[:, c, :], ACT.Sigmoid, n=TT,
                     extra=lambda src: A_(kk[:, c, :], src, ACT.Sigmoid, scale=-1.0))
            act.wait_ge(S("f_ready"), 1)
            A_(sf, sf, ACT.Ln).then_inc(S("logf"), 1)
            for c in range(4):
                evac(qx[:, c, :], ACT.Copy, n=T)
            for part in range(2):
                act.wait_ge(S("end_diff"), part + 1)
                n = (META, P)[part]
                A_(W[part].rearrange("p (c t) -> p c t", c=4)[:, :, 0:n],
                   W[part].rearrange("p (c t) -> p c t", c=4)[:, :, 0:n], ACT.Exp).then_inc(S("end_decay"), 1)
            A_(egA, Gx[:, :, P - 1:P].rearrange("p c t -> p (c t)"), ACT.Exp).then_inc(S("eg"), 1)

            def level_exp(l):
                act.wait_ge(S("diff"), l + 1)
                A_(W[l % 2], W[l % 2], ACT.Exp).then_inc(S("decay"), 1)

            for c in range(4):
                evac(lx[:, c, 3:3 + TT], ACT.Copy, n=TT)
            level_exp(0)
            level_exp(1)
            for c in range(4):
                evac(lx[:, 4 + c, 3:3 + TT], ACT.Copy, n=TT)
            level_exp(2)
            level_exp(3)
            for c in range(4):
                evac(ly[:, c, :], ACT.Gelu_apprx_tanh, n=T)
            level_exp(4)
            level_exp(5)
            for c in range(4):
                evac(ly[:, 4 + c, :], ACT.Gelu_apprx_tanh, n=T)
            level_exp(6)
            for c in range(4):
                evac(og[:, c, :], ACT.Sigmoid, n=T)
            act.wait_ge(S("diff"), 8)
            A_(W[1], Gx.rearrange("p c t -> p (c t)"), ACT.Exp).then_inc(S("decay"), 1)
            for c in range(4):
                evac(ga[:, c, :], ACT.Sigmoid, n=T)
            act.wait_ge(S("o_ready"), 1)
            for c in range(2):
                A_(oT.rearrange("p c t -> p (c t)")[:, 512 * c:512 * c + 512], bank[4 + c][:, :], ACT.Copy)
                A_(W[0][:, 512 * c:512 * c + 512], bank[4 + c][:, :], ACT.Square).then_inc(S("o_squared"), 1)
            for c in range(4):
                evac(ga[:, 4 + c, :], ACT.Sigmoid, n=T)
            act.wait_ge(S("o_mean"), 1)
            A_(rsn, rsn, ACT.Sqrt).then_inc(S("o_root"), 1)
            for b in range(KC):
                for q in range(2):
                    n = 2 * b + q
                    act.wait_ge(S("lru_products"), n + 1)
                    A_((lrur, lrui)[q][:, b, :], bank[4 + n % 4][:, 0:TT], ACT.Sigmoid,
                       bias=V(("lru_b_r", "lru_b_i")[q], b)).then_inc(S("lru_gates"), 1)
            for c in range(4):
                evac(gb[:, c, :], ACT.Sigmoid, n=T)
            act.wait_ge(S("lru_gates"), 16)
            act.wait_ge(S("sp_ready"), 1)
            act.wait_ge(S("oa_ready"), 1)
            for b in range(KC):
                A_(lrua[:, b, :], lrur[:, b, :], ACT.Exp, scale=m2sp[:, b:b + 1])
            for b in range(KC):
                last = A_(lrur[:, b, :], lrur[:, b, :], ACT.Tanh, scale=sp8[:, b:b + 1])
            last.then_inc(S("lru_decays"), 1)
            act.wait_ge(S("lru_under"), 1)
            A_(lrut, lrut, ACT.Sqrt).then_inc(S("lru_root"), 1)
            for c in range(4):
                evac(gb[:, 4 + c, :], ACT.Sigmoid, n=T)

            act.wait_ge(S("out_merged"), 2)
            act.dma_start(g2b, A["norm2_g"].partition_broadcast(P).rearrange("p a b -> p (a b)")).then_inc(S("g2_loaded"), 16)
            act.dma_start(fgb, A["final_g"].rearrange("(a b) -> a b", a=1).partition_broadcast(P)
                          .rearrange("p a b -> p (a b)")).then_inc(S("fg_loaded"), 16)
            act.dma_start(rw[:, :, 0:4], A["w_group"][0].rearrange("(k p) e -> p k e", p=P)).then_inc(S("rw_loaded"), 16)
            for g in range(GROUPS):
                act.dma_start(rw[:, :, 4 + EPG * g:4 + EPG * (g + 1)],
                              A["w_router"][0, g].rearrange("(k p) e -> p k e", p=P)).then_inc(S("rw_loaded"), 16)
            squares("n2", ((0, P, ("h_added", 1)), (1, P, ("h_added", 2))), h, hf, 24)
            for t in range(NT):
                act.wait_ge(S("norm_rows"), ROWS["n2"] + t + 1)
                act.dma_start(hf_d[t * P:(t + 1) * P, :], hf[:, t, :]).then_inc(S("hf_stored"), 16)
            act.wait_ge(S("route_diff"), 1)
            A_(rt[:, 64:72], rt[:, 64:72], ACT.Exp).then_inc(S("route_exp"), 1)
            act.wait_ge(S("route_diff2"), 1)
            A_(rt[:, 80:82], rt[:, 80:82], ACT.Exp).then_inc(S("route_exp"), 1)

            def silu():
                return A_(sg, bank[0][:, :], ACT.Silu)

            def copy_turned():
                return A_(xgT[:, 0:4, :], bank[2][:, 0:8 * CAP], ACT.Copy)

            def copy_hidden():
                return A_(hT, bank[6][:, :], ACT.Copy)

            act.wait_ge(S("rows_turned"), 1)
            copy_turned().then_inc(S("turned_copied"), 1)

            def pair(i, last_pair):
                act.wait_ge(S("gates"), i + 1)
                not_zero(act, "hidden", i)
                silu().then_inc(S("silu"), 1)
                if not last_pair:
                    act.wait_ge(S("rows_turned"), i + 2)
                    copy_turned().then_inc(S("turned_copied"), 1)
                act.wait_ge(S("hid_turned"), i + 1)
                copy_hidden().then_inc(S("hT_ready"), 1)
                act.wait_ge(S("y_ready"), i + 1)
                not_zero(act, "y_stored", 16 * i)
                A_(ysb[:, 0:512], bank[4][:, :], ACT.Copy).then_inc(S("y_copied"), 1)
                act.wait_ge(S("y_copied"), 2 * i + 2)
                act.dma_start(y_d[bass.ds(i * 2 * CAP, 2 * CAP), :], ysb).then_inc(S("y_stored"), 16)

            pair(0, False)
            with act.Fori(1, PAIRS - 1) as i:
                pair(i, False)
            pair(PAIRS - 1, True)
            act.wait_ge(S("flag_set"), 1)
            over = act.value_load(idx[0:1, 40:41], min_val=0, max_val=T)
            with act.If(over > CAP):
                act.wait_ge(S("y_stored"), 16 * PAIRS)
                with act.Fori(0, (PASSES - 1) * PAIRS) as n:
                    act.wait_ge(S("over_turned"), n + 1)
                    copy_turned().then_inc(S("over_half"), 1)
                    act.wait_ge(S("over_gate_up"), n + 1)
                    silu().then_inc(S("over_silu"), 1)
                    act.wait_ge(S("over_hid"), n + 1)
                    copy_hidden().then_inc(S("over_hT"), 1)
                    act.wait_ge(S("over_y"), n + 2)
                    A_(ysb[:, 0:512], bank[4][:, :], ACT.Copy).then_inc(S("over_copied"), 1)
                    act.wait_ge(S("over_copied"), 2 * n + 2)
                    act.dma_start(y_d[bass.ds(SLOTS + n * 2 * CAP, 2 * CAP), :], ysb).then_inc(S("over_stored"), 16)
                act.wait_ge(S("over_stored"), 16 * (PASSES - 1) * PAIRS)

            squares("f1", ((0, P, ("y_added", 1)), (1, P, ("y_added", 2))), h, hf, 48)
            squares("n3", ((0, P, ("x2_ready", 1)), (1, P, ("x2_ready", 2))), h, xn2, 50)
            act.wait_ge(S("angles"), 1)
            A_(rt[:, 0:32], rt[:, 0:32], ACT.Sin).then_inc(S("sincos"), 1)
            for n in range(6):
                for t in range(NT):
                    if n >= 2:
                        act.wait_ge(S("qk_turned"), 2 * (n - 1))
                    elif n == 0:
                        act.wait_ge(S("norm_done"), 2 * ROWS["n3"] + 4)
                    evac(qk[n % 2][:, t, :], ACT.Copy)
                if n >= 1:
                    for t in range(NT):
                        m = 2 * (n - 1) + t
                        act.wait_ge(S("qk_turned"), m + 1)
                        A_(qkT[:, 4 * (n - 1):4 * n, t * P:(t + 1) * P], bank[4 + m % 4][:, :]
                           .rearrange("p (c t) -> p c t", c=4), ACT.Copy).then_inc(S("qk_copied"), 1)
            for g in range(NG):
                for t in range(NT):
                    evac(vv[:, t, 512 * g:512 * g + 512], ACT.Copy)
                if g == 0:
                    for t in range(NT):
                        m = 10 + t
                        act.wait_ge(S("qk_turned"), m + 1)
                        A_(qkT[:, 20:24, t * P:(t + 1) * P], bank[4 + m % 4][:, :]
                           .rearrange("p (c t) -> p c t", c=4), ACT.Copy).then_inc(S("qk_copied"), 1)
            act.wait_ge(S("x2_ready"), NT)
            act.dma_start(wsr.rearrange("p (g t) -> p g t", g=SG), A["w_spatial_2"][0].rearrange("g t s -> t g s")) \
                .then_inc(S("ws_loaded"), 16)
            act.wait_ge(S("qk_turned"), 12)
            act.dma_start(lngb[:, 0:512], A["sgu_ln_g_2"].partition_broadcast(P).rearrange("p a b -> p (a b)")).then_inc(S("ln_loaded"), 16)
            act.dma_start(lngb[:, 512:1024], A["sgu_ln_b_2"].partition_broadcast(P).rearrange("p a b -> p (a b)")).then_inc(S("ln_loaded"), 16)
            for u in range(2):
                for t in range(NT):
                    evac(uv[:, t, 512 * u:512 * u + 512], ACT.Gelu)

            def gate_evac():
                c = n_out[0] - GATE0
                evac(gate[:, c, :], ACT.Sigmoid, n=T, b=c % 2)

            GATE0 = n_out[0]

            def exp_scores(n):
                keys = NG * (T if n % 2 == 0 else P)
                c = 100 + 4 * (n % 2)
                act.wait_ge(S("scored"), n + 1)
                A_(sc[n % 2][:, 0:keys], sc[n % 2][:, 0:keys], ACT.Exp, scale=HD ** -0.5, bias=stat[:, c:c + 1],
                   accum_out=stat[:, c + 1:c + 2]).then_inc(S("probs"), 1)

            exp_scores(0)
            for n in range(2 * AH):
                tile = 1 - n % 2
                gate_evac()
                act.wait_ge(S("probs_turned"), n + 1)
                if n >= 1:
                    act.wait_ge(S("pv"), n)
                w = 512 if tile else NG * P
                A_(PTb[:, 0:w], bank[2][:, 0:w], ACT.Copy).then_inc(S("PT_half" if tile else "PT_ready"), 1)
                if n + 1 < 2 * AH:
                    exp_scores(n + 1)
            squares("n4", ((0, P, ("x3_added", 1)), (1, P, ("x3_added", 2))), h, xn2, 64)
            for c in range(FC):
                act.wait_ge(S("ff"), c + 1)
                if c >= 4:
                    act.wait_ge(S("ff_cols"), c - 3)
                A_(sgf[:, c % 4, :], bank[4 + c % 4][:, 0:T], ACT.Silu).then_inc(S("ff_silu"), 1)
                if c == 4:
                    act.dma_start(fgb2, A["final_g_2"].rearrange("(a b) -> a b", a=1).partition_broadcast(P)
                                  .rearrange("p a b -> p (a b)")).then_inc(S("fg2_loaded"), 16)
            squares("f2", ((0, P, ("x4_added", 1)), (1, P, ("x4_added", 2))), h, outr, 88)

        @block.vector
        def _(dve):
            v = nc.vector
            n_link = [0]

            def link(ins):
                n_link[0] += 1
                ins.then_inc(S("dve_chain"), 1)
                dve.wait_ge(S("dve_chain"), n_link[0])

            def norm_rows(name, order, src, dst, col, g=None):
                for j, (tile, n) in enumerate(order):
                    dve.wait_ge(S("norm_rstd"), STATS[name] + j + 1)
                    r = stat[0:n, col + 16 + tile:col + 17 + tile]
                    if g is None:
                        rows = src[0:n, tile, :] if tile < NT else meta[0:n, :]
                        v.tensor_scalar(dst[0:n, tile, :], rows, r, None, ALU.mult) \
                            .then_inc(S("norm_rows"), 1)
                    else:
                        v.scalar_tensor_tensor(out=dst[0:n, tile, :], in0=src[0:n, tile, :], scalar=r, in1=g,
                                               op0=ALU.mult, op1=ALU.mult).then_inc(S("norm_rows"), 1)

            def turned_out(name, order, dst, g):
                for j, (lo, n) in enumerate(order):
                    for half in range(2):
                        dve.wait_ge(S("norm_turned"), 2 * ROWS[name] + 2 * j + half + 1)
                        src = bank[2 * j + half][:, 0:4 * n].rearrange("p (c t) -> p c t", c=4)
                        o = dst[:, 4 * half:4 * half + 4, lo:lo + n]
                        if g is None:
                            v.tensor_copy(o, src).then_inc(S("norm_done"), 1)
                        else:
                            v.tensor_tensor(o, src, bc(V(g, 4 * half, 4), [P, 4, n], 2), ALU.mult) \
                                .then_inc(S("norm_done"), 1)

            dve.wait_ge(S("vec_turned"), 1)
            link(v.tensor_copy(vec[:, :], bank[7][:, 0:NVR]))
            norm_rows("n1", ((2, META), (0, P), (1, P)), h, xn, 0)
            turned_out("n1", ((0, META), (META, P), (META + P, P)), hnT, "norm1_g")

            v.tensor_tensor(lbv, V("hg_lower_bounds", 4, 4), V("hg_lower_bounds", 0, 4), ALU.subtract) \
                .then_inc(S("lb_diff"), 1)
            dve.wait_ge(S("lb_exp"), 1)
            link(v.tensor_scalar(omlb, lbv, 1.0, None, ALU.add))
            link(v.reciprocal(lbv, omlb))
            link(v.tensor_scalar(omlb, lbv, -1.0, 1.0, ALU.mult, ALU.add))
            lam = V("lru_lambda", 0, 8)
            link(v.tensor_scalar(tmp8, lam, -1.0, None, ALU.mult))
            v.tensor_tensor(m2sp, tmp8, lam, ALU.min).then_inc(S("lam_abs"), 1)
            link(v.tensor_scalar(tmp8, tmp8, 0.0, None, ALU.max))
            dve.wait_ge(S("sp_log"), 1)
            link(v.tensor_tensor(tmp8, tmp8, m2sp, ALU.add))
            v.tensor_scalar(sp8, tmp8, 8.0, None, ALU.mult)
            v.tensor_scalar(m2sp, tmp8, -8.0, None, ALU.mult).then_inc(S("sp_ready"), 1)

            dve.wait_ge(S("iotas"), 2)
            link(v.tensor_tensor(maskw[:, 6, :], idx[:, 60:61].to_broadcast([P, P]), maskw[:, 7, :], ALU.bitwise_xor))
            link(v.tensor_tensor(maskw[:, 5, :], maskw[:, 7, :], idx[:, 60:61].to_broadcast([P, P]), ALU.is_gt))
            link(v.tensor_copy(maskw[:, 7, :], maskw[:, 6, :]))
            link(v.tensor_copy(PT[:, 7, :].bitcast(I32), maskw[:, 5, :]))
            tgt = PT[:, 7, :].bitcast(I32)
            for l, m in enumerate(LEVELS):
                link(v.tensor_scalar(maskw[:, l, :], maskw[:, 7, :], m, None, ALU.is_ge))
                link(v.tensor_tensor(maskw[:, l, :], maskw[:, l, :], tgt, ALU.mult))
                link(v.tensor_scalar(PT[:, 6, :].bitcast(I32), maskw[:, 7, :], 2 * m, None, ALU.is_lt))
                link(v.tensor_tensor(maskw[:, l, :], maskw[:, l, :], PT[:, 6, :].bitcast(I32), ALU.mult))
            link(v.tensor_scalar(maskw[:, 7, :], maskw[:, 7, :], 0, None, ALU.is_equal))
            dve.wait_ge(S("pool_chain"), 5)
            link(v.memset(PT, 0.0))

            dve.wait_ge(S("evac"), 7)
            for c in range(HEADS):
                last = v.tensor_scalar(sf[:, c, :], sf[:, c, :], omlb[:, c:c + 1], lbv[:, c:c + 1],
                                       ALU.mult, ALU.add)
            last.then_inc(S("f_ready"), 1)
            for c in range(HEADS):
                last = v.tensor_scalar(kk[:, c, :], kk[:, c, :], omlb[:, c:c + 1], None, ALU.mult)
            link(last)
            link(v.tensor_copy(kx, kk[:, :, META:TT]))
            dve.wait_ge(S("logf"), 1)
            for c in range(HEADS):
                v.tensor_tensor_scan(Gm[:, c, :], ones[:, 0:META], sf[:, c, 0:META], 0.0, ALU.mult, ALU.add)
                for t in range(NT):
                    last = v.tensor_tensor_scan(Gx[:, c, t * P:(t + 1) * P], ones[:, :],
                                                sf[:, c, META + t * P:META + (t + 1) * P], 0.0, ALU.mult, ALU.add)
            link(last)
            for part in range(2):
                n = (META, P)[part]
                G = (Gm, Gx)[part]
                k = (kk, kx)[part]
                d = W[part].rearrange("p (c t) -> p c t", c=4)[:, :, 0:n]
                v.tensor_tensor(d, G[:, :, n - 1:n].to_broadcast([P, 4, n]), G[:, :, 0:n], ALU.subtract) \
                    .then_inc(S("end_diff"), 1)
            for part in range(2):
                n = (META, P)[part]
                k = (kk, kx)[part]
                d = W[part].rearrange("p (c t) -> p c t", c=4)[:, :, 0:n]
                dve.wait_ge(S("end_decay"), part + 1)
                v.tensor_tensor(kE[:, 0:512].rearrange("p (c t) -> p c t", c=4)[:, :, 0:n], k[:, :, 0:n], d, ALU.mult) \
                    .then_inc(S("k_end"), 1)
                dve.wait_ge(S("k_turned"), part + 1)
                v.tensor_copy(kT[0:n, part, :], bank[4][0:n, :]).then_inc(S("kT_ready"), 1)
                dve.wait_ge(S("kv"), part + 1)
                if part == 0:
                    v.tensor_copy(St[:, 0, :, :], bank[5][:, :].rearrange("p (h v) -> p h v", h=4)) \
                        .then_inc(S("state"), 1)
                else:
                    dve.wait_ge(S("eg"), 1)
                    dve.wait_ge(S("state"), 1)
                    for hd in range(HEADS):
                        last = v.scalar_tensor_tensor(out=St[:, 1, hd, :], in0=St[:, 0, hd, :],
                                                      scalar=egA[:, hd:hd + 1], in1=bank[5][:, hd * P:(hd + 1) * P],
                                                      op0=ALU.mult, op1=ALU.add)
                    last.then_inc(S("state"), 1)

            def seg(ap, m):
                return ap.rearrange("p (n w) -> p n w", w=2 * m)

            Gf = Gx.rearrange("p c t -> p (c t)")
            qf = qx.rearrange("p c t -> p (c t)")
            kf = kx.rearrange("p c t -> p (c t)")

            def diff(l):
                m = LEVELS[l]
                n = 512 // m
                mid = seg(Gf, m)[:, :, m - 1:m].to_broadcast([P, n, m])
                w = seg(W[l % 2], m)
                v.tensor_tensor(w[:, :, m:2 * m], seg(Gf, m)[:, :, m:2 * m], mid, ALU.subtract)
                v.tensor_tensor(w[:, :, 0:m], mid, seg(Gf, m)[:, :, 0:m], ALU.subtract).then_inc(S("diff"), 1)

            def scaled(l):
                m = LEVELS[l]
                dve.wait_ge(S("decay"), l + 1)
                if l >= 2:
                    dve.wait_ge(S("levels"), l - 1)
                w = seg(W[l % 2], m)
                o = seg(z[l % 2], m)
                v.tensor_tensor(o[:, :, m:2 * m], seg(qf, m)[:, :, m:2 * m], w[:, :, m:2 * m], ALU.mult)
                v.tensor_tensor(o[:, :, 0:m], seg(kf, m)[:, :, 0:m], w[:, :, 0:m], ALU.mult).then_inc(S("z_ready"), 1)

            def pick(l):
                dve.wait_ge(S("levels"), l + 1)
                if l:
                    dve.wait_ge(S("picked"), l)
                for b in range(2):
                    last = v.copy_predicated(PT[:, 4 * b:4 * b + 4, :],
                                             bc(maskw[:, l, :], [P, 4, P], 1),
                                             bank[4 + 2 * (l % 2) + b][:, :].rearrange("p (c t) -> p c t", c=4))
                last.then_inc(S("picked"), 1)

            dve.wait_ge(S("evac"), 11)
            dve.wait_ge(S("k_end"), 2)
            dve.wait_ge(S("k_turned"), 2)
            diff(0)
            for l in range(7):
                if l < 6:
                    if l >= 1:
                        dve.wait_ge(S("z_ready"), l)
                    diff(l + 1)
                scaled(l)
                if l >= 1:
                    pick(l - 1)
            v.memset(pdt[:, 1:2], 0.0).then_inc(S("diff"), 1)
            pick(6)
            pick(7)
            dve.wait_ge(S("decay"), 8)
            v.tensor_tensor(qf, qf, W[1], ALU.mult).then_inc(S("qe_ready"), 1)

            for c in range(KC):
                dve.wait_ge(S("evac"), 12 + c)
                link(v.tensor_scalar(xc[:, c, :], lx[:, c, 0:TT], V("conv_w", c), V("conv_b", c), ALU.mult, ALU.add))
                for j in range(1, 4):
                    ins = v.scalar_tensor_tensor(out=xc[:, c, :], in0=lx[:, c, j:j + TT],
                                                 scalar=V("conv_w", 8 * j + c), in1=xc[:, c, :],
                                                 op0=ALU.mult, op1=ALU.add)
                    if j < 3:
                        link(ins)
                    else:
                        ins.then_inc(S("conv"), 1)
            of = oT.rearrange("p c t -> p (c t)")
            dve.wait_ge(S("o_sums"), 1)
            for c in range(2):
                last = v.tensor_scalar(rsn[:, 512 * c:512 * c + 512], bank[6 + c][:, :], 1.0 / P, EPS, ALU.mult, ALU.add)
            last.then_inc(S("o_mean"), 1)
            dve.wait_ge(S("o_mean"), 1)
            dve.wait_ge(S("o_root"), 1)
            link(v.reciprocal(rsn, rsn))
            dve.wait_ge(S("o_squared"), 2)
            link(v.tensor_tensor(of, of, rsn, ALU.mult))
            for c in range(HEADS):
                last = v.scalar_tensor_tensor(out=oT[:, c, :], in0=oT[:, c, :], scalar=V("hg_norm_g", c),
                                              in1=og[:, c, :], op0=ALU.mult, op1=ALU.mult)
            last.then_inc(S("oa_ready"), 1)
            dve.wait_ge(S("lru_decays"), 1)
            link(v.tensor_tensor(lrut, lrua, lrua, ALU.mult))
            for c in range(2):
                last = v.scalar_tensor_tensor(out=lrut[:, 4 * c:4 * c + 4, :], in0=lrut[:, 4 * c:4 * c + 4, :],
                                              scalar=1.0, in1=lrur[:, 4 * c:4 * c + 4, :], op0=ALU.add, op1=ALU.mult)
            last.then_inc(S("lru_under"), 1)
            link(v.tensor_tensor(lrui, lrui, xc, ALU.mult))
            dve.wait_ge(S("lru_root"), 1)
            link(v.tensor_tensor(lrui, lrui, lrut, ALU.mult))
            for c in range(KC):
                last = v.tensor_tensor_scan(lrut[:, c, :], lrua[:, c, :], lrui[:, c, :], 0.0, ALU.mult, ALU.add)
            link(last)
            dve.wait_ge(S("evac"), 27)
            v.tensor_tensor(ly, ly, lrut[:, :, META:TT], ALU.mult).then_inc(S("ob_ready"), 1)

            def merge(name_a, name_b, done, ga_, gb_, dst, tmp):
                dve.wait_ge(S(name_a), 1)
                for m in range(KC):
                    dve.wait_ge(S(name_b), 2 * (m // 2) + 2)
                    cols = slice((m % 2) * T, (m % 2 + 1) * T)
                    v.tensor_tensor(tmp[:, 0:T], ga_[:, m, :], bank[m // 2][:, cols], ALU.mult)
                    link(v.tensor_tensor(tmp[:, T:2 * T], gb_[:, m, :], bank[4 + m // 2][:, cols], ALU.mult))
                    v.tensor_tensor(dst[:, m, :], tmp[:, 0:T], tmp[:, T:2 * T], ALU.add).then_inc(S(done), 1)
                    dve.wait_ge(S(done), m + 1)

            dve.wait_ge(S("evac"), 47)
            merge("up_a", "up_b", "merged", ga, gb, mT, W[0])

            def add_rows(ready, done):
                for t in range(NT):
                    for half in range(2):
                        hh = h[:, t, half * 512:(half + 1) * 512]
                        ins = v.tensor_tensor(hh, hh, bank[2 * t + half][:, :], ALU.add)
                    ins.then_inc(S(done), 1)

            dve.wait_ge(S("out_merged"), 2)
            add_rows("out_merged", "h_added")
            dve.wait_ge(S("g2_loaded"), 16)
            norm_rows("n2", ((0, P), (1, P)), h, hf, 24, g=g2b)
            turned_out("n2", ((0, P), (P, P)), hfT, None)

            dve.wait_ge(S("logits"), 2)
            dve.wait_ge(S("bias_loaded"), 32)
            dve.wait_ge(S("route_consts"), 4)
            for t in range(NT):
                last = v.tensor_tensor(lg[:, t, :], bank[4 + t][:, 0:36], bias36, ALU.add)
            link(last)
            o = [100]

            def r2(n):
                a = rt[:, o[0]:o[0] + 2 * n].rearrange("p (t e) -> p t e", t=2)
                o[0] += 2 * n
                return a

            def one_hot(dst, vals, n, scratch, vmax, vidx):
                io = bc(iota32[:, 0:n], [P, 2, n], 1)
                link(v.tensor_reduce(vmax, vals, AX_X, ALU.max))
                link(v.tensor_tensor(scratch, vals, vmax.to_broadcast([P, 2, n]), ALU.is_lt))
                link(v.scalar_tensor_tensor(out=scratch, in0=scratch, scalar=1000.0, in1=io, op0=ALU.mult, op1=ALU.add))
                link(v.tensor_reduce(vidx, scratch, AX_X, ALU.min))
                link(v.tensor_tensor(dst, vidx.to_broadcast([P, 2, n]), io, ALU.is_equal))

            gm, gi, m1, i1, m2, i2 = (r2(1) for _ in range(6))
            goh, gs = r2(4), r2(4)
            one_hot(goh, lg[:, :, 0:4], 4, gs, gm, gi)
            ge = rt[:, 64:72].rearrange("p (t e) -> p t e", t=2)
            v.tensor_tensor(ge, lg[:, :, 0:4], gm.to_broadcast([P, 2, 4]), ALU.subtract).then_inc(S("route_diff"), 1)
            big, es, e1, e2 = r2(32), r2(32), r2(32), r2(32)
            big4 = big.rearrange("p t (g e) -> p t g e", g=GROUPS)
            for t in range(NT):
                last = v.tensor_scalar(big4[:, t], bc(goh[:, t, :], [P, GROUPS, EPG], 2), -1.0, -NEG, ALU.add, ALU.mult)
            link(last)
            for t in range(NT):
                last = v.tensor_tensor(es[:, t].rearrange("p (g e) -> p g e", g=GROUPS),
                                       lg[:, t, 4:36].rearrange("p (g e) -> p g e", g=GROUPS),
                                       bc(goh[:, t, :], [P, GROUPS, EPG], 2), ALU.mult)
            link(last)
            link(v.tensor_tensor(big, big, es, ALU.add))
            one_hot(e1, big, 32, es, m1, i1)
            link(v.scalar_tensor_tensor(out=big, in0=e1, scalar=2.0 * NEG, in1=big, op0=ALU.mult, op1=ALU.add))
            one_hot(e2, big, 32, es, m2, i2)
            M = rt[:, 0:64].rearrange("p (t e) -> p t e", t=2)
            v.tensor_tensor(M, e1, e2, ALU.add).then_inc(S("chosen"), 1)
            dd = rt[:, 80:82].rearrange("p (t e) -> p t e", t=2)
            v.tensor_tensor(dd, m2, m1, ALU.subtract).then_inc(S("route_diff2"), 1)
            dve.wait_ge(S("places"), 1)
            rank = r2(32)
            link(v.tensor_copy(rank.rearrange("p t e -> p (t e)"), bank[6][:, 0:64]))
            cnt = r2(1)
            link(v.tensor_reduce(cnt[:, 0, :], bank[6][:, 64:96], AX_X, ALU.max))
            v.tensor_copy(idx[:, 40:41], cnt[:, 0, :]).then_inc(S("flag_set"), 1)
            s1, s2, p1, sl, ps_ = r2(32), r2(1), r2(1), r2(1), r2(1)
            for j, eo in enumerate((e1, e2)):
                link(v.tensor_tensor(s1, eo, rank, ALU.mult))
                link(v.tensor_reduce(s2, s1, AX_X, ALU.add))
                link(v.tensor_scalar(ps_, s2, float(CAP), None, ALU.is_ge))
                for a in range(2, PASSES):
                    link(v.scalar_tensor_tensor(out=ps_, in0=s2, scalar=float(CAP * a), in1=ps_, op0=ALU.is_ge, op1=ALU.add))
                for q, (base, mul, per) in enumerate(((base_l, PAIRS, SLOTS - PAIRS * CAP), (base_s, 1, SLOTS - CAP))):
                    link(v.tensor_tensor(s1, eo, bc(base, [P, 2, 32], 1), ALU.mult))
                    link(v.tensor_reduce(p1, s1, AX_X, ALU.add))
                    link(v.scalar_tensor_tensor(out=p1, in0=s2, scalar=float(mul), in1=p1, op0=ALU.mult, op1=ALU.add))
                    link(v.scalar_tensor_tensor(out=sl, in0=ps_, scalar=float(per), in1=p1, op0=ALU.mult, op1=ALU.add))
                    v.tensor_copy(idx[:, 4 * q + j:4 * q + j + 3:2], sl.rearrange("p t e -> p (t e)")) \
                        .then_inc(S("slots_set"), 1)
            dve.wait_ge(S("route_exp"), 2)
            wt = rt[:, 84:88].rearrange("p (t k) -> p t k", t=2)
            link(v.tensor_reduce(p1, ge, AX_X, ALU.add))
            link(v.tensor_scalar(s2, dd, 1.0, None, ALU.add))
            link(v.tensor_tensor(s2, s2, p1, ALU.mult))
            link(v.reciprocal(wt[:, :, 0:1], s2))
            link(v.tensor_tensor(wt[:, :, 1:2], wt[:, :, 0:1], dd, ALU.mult))

            def copy_turned():
                return v.tensor_copy(xgT[:, 4:8, :], bank[3][:, 0:8 * CAP].rearrange("p (c t) -> p c t", c=4))

            def hidden():
                return v.tensor_tensor(hid, sg, bank[1][:, :], ALU.mult)

            dve.wait_ge(S("rows_turned"), 1)
            copy_turned().then_inc(S("turned_copied"), 1)

            def pair(i, last_pair):
                dve.wait_ge(S("silu"), i + 1)
                dve.wait_ge(S("ups"), i + 1)
                hidden().then_inc(S("hidden"), 1)
                if not last_pair:
                    dve.wait_ge(S("rows_turned"), i + 2)
                    copy_turned().then_inc(S("turned_copied"), 1)
                dve.wait_ge(S("y_ready"), i + 1)
                not_zero(dve, "y_stored", 16 * i)
                v.tensor_copy(ysb[:, 512:1024], bank[5][:, :]).then_inc(S("y_copied"), 1)

            pair(0, False)
            with dve.Fori(1, PAIRS - 1) as i:
                pair(i, False)
            pair(PAIRS - 1, True)
            dve.wait_ge(S("flag_set"), 1)
            over = dve.value_load(idx[0:1, 40:41], min_val=0, max_val=T)
            with dve.If(over > CAP):
                with dve.Fori(0, (PASSES - 1) * PAIRS) as n:
                    dve.wait_ge(S("over_half"), n + 1)
                    copy_turned().then_inc(S("over_xgT"), 1)
                    dve.wait_ge(S("over_silu"), n + 1)
                    hidden().then_inc(S("over_hidden"), 1)
                    dve.wait_ge(S("over_y"), n + 2)
                    v.tensor_copy(ysb[:, 512:1024], bank[5][:, :]).then_inc(S("over_copied"), 1)

            dve.wait_ge(S("y_back"), 64)
            for t in range(NT):
                link(v.scalar_tensor_tensor(out=h[:, t, :], in0=yg[:, 2 * t, :], scalar=wt[:, t, 0:1], in1=h[:, t, :],
                                            op0=ALU.mult, op1=ALU.add))
                v.scalar_tensor_tensor(out=h[:, t, :], in0=yg[:, 2 * t + 1, :], scalar=wt[:, t, 1:2], in1=h[:, t, :],
                                       op0=ALU.mult, op1=ALU.add).then_inc(S("y_added"), 1)
            dve.wait_ge(S("fg_loaded"), 16)
            for t in range(NT):
                dve.wait_ge(S("norm_rstd"), STATS["f1"] + t + 1)
                v.scalar_tensor_tensor(out=h[:, t, :], in0=h[:, t, :], scalar=stat[:, 64 + t:65 + t], in1=fgb,
                                       op0=ALU.mult, op1=ALU.mult).then_inc(S("x2_ready"), 1)
            dve.wait_ge(S("pos_loaded"), 16)
            dve.wait_ge(S("y_back"), 64)
            dve.wait_ge(S("list_put"), 64)
            link(v.tensor_copy(pdt[:, 6:8], idx[:, 56:58]))
            ang = rt[:, 0:32].rearrange("p (q t f) -> p q t f", q=2, t=2)
            trn = rt[:, 32:64].rearrange("p (q t f) -> p q t f", q=2, t=2)
            for q in range(2):
                for f in range(8):
                    last = v.tensor_scalar(ang[:, q, :, f], pdt[:, 6:8], INV_FREQ[f], None, ALU.mult)
            link(last)
            MAGIC = 12582912.0
            C1, C2, C3 = 6.28125, 0.0019350051879882812, 3.0197e-07
            two_pi = 2 * np.pi
            C3 = float(np.float32(two_pi - C1 - C2))
            for q in range(2):
                link(v.tensor_scalar(trn[:, q], ang[:, q], float(1 / two_pi), 0.25 * (1 - q), ALU.mult, ALU.add))
            link(v.tensor_scalar(trn, trn, MAGIC, None, ALU.add))
            link(v.tensor_scalar(trn, trn, -MAGIC, None, ALU.add))
            for C in (C1, C2, C3):
                for q in range(2):
                    last = v.scalar_tensor_tensor(out=ang[:, q], in0=trn[:, q], scalar=-C, in1=ang[:, q],
                                                  op0=ALU.mult, op1=ALU.add)
                link(last)
            link(v.tensor_scalar(ang[:, 0], ang[:, 0], float(np.pi / 2), None, ALU.add))
            v.tensor_scalar(rt[:, 0:32], rt[:, 0:32], 3.1415925, -3.1415925, ALU.min, ALU.max).then_inc(S("angles"), 1)

            norm_rows("n3", ((0, P), (1, P)), h, xn2, 50)
            turned_out("n3", ((0, P), (P, P)), hn2, "norm1_g_2")

            dve.wait_ge(S("diff_iota"), 1)
            di = scw[:, 0:T].bitcast(I32)
            lowi = scw[:, T:2 * T].bitcast(I32)
            lowf = scw[:, 2 * T:3 * T]
            for g, dil in ((1, 4), (2, 16)):
                link(v.tensor_scalar(lowi, di, dil - 1, None, ALU.bitwise_and))
                link(v.tensor_scalar(lowf, lowi, 0.0, NEG, ALU.is_gt, ALU.mult))
                for o_, n in ((T * g, T), (NG * T + P * g, P)):
                    link(v.tensor_tensor(amask[:, o_:o_ + n], amask[:, o_:o_ + n], lowf[:, 0:n], ALU.add))

            dve.wait_ge(S("sincos"), 1)
            cos = ang[:, 0]
            sin = ang[:, 1]
            for n in range(6):
                dve.wait_ge(S("evac"), 47 + 2 * n + 2)
                for t in range(NT):
                    x = qk[n % 2][:, t, :].rearrange("p (h d) -> p h d", h=AH)
                    x1, x2 = x[:, :, 0:8], x[:, :, 8:16]
                    c8 = bc(cos[:, t, :], [P, AH, 8], 1)
                    s8 = bc(sin[:, t, :], [P, AH, 8], 1)
                    a, b, c, d = (rtmp[:, k, 64 * t:64 * t + 64].rearrange("p (h d) -> p h d", h=AH) for k in range(4))
                    v.tensor_tensor(a, x1, c8, ALU.mult)
                    v.tensor_tensor(b, x2, s8, ALU.mult)
                    v.tensor_tensor(c, x2, c8, ALU.mult)
                    link(v.tensor_tensor(d, x1, s8, ALU.mult))
                    v.tensor_tensor(x1, a, b, ALU.subtract)
                    last = v.tensor_tensor(x2, c, d, ALU.add)
                last.then_inc(S("roped"), 1)

            dve.wait_ge(S("ws_turned"), 1)
            for g2 in range(2):
                v.tensor_copy(wsT[:, 4 * g2:4 * g2 + 4, :], bank[4 + g2][:, :].rearrange("p (g t) -> p g t", g=4)) \
                    .then_inc(S("ws_ready"), 1)
            dve.wait_ge(S("evac"), 47 + 22)
            bn = rt[:, 64:80].rearrange("p (t n) -> p t n", t=2)
            for t in range(NT):
                link(v.bn_stats(bn[:, t, 0:6], uv[:, t, 512:1024]))
                link(v.bn_aggr(bn[:, t, 6:8], bn[:, t, 0:6]))
                v.tensor_copy(stat[:, 56 + t:57 + t], bn[:, t, 7:8]).then_inc(S("norm_sums"), 1)
            dve.wait_ge(S("ln_loaded"), 32)
            for t in range(NT):
                dve.wait_ge(S("norm_rstd"), STATS["ln"] + t + 1)
                x = uv[:, t, 512:1024]
                link(v.tensor_scalar(x, x, bn[:, t, 6:7], stat[:, 72 + t:73 + t], ALU.subtract, ALU.mult))
                link(v.tensor_tensor(x, x, lngb[:, 0:512], ALU.mult))
                v.tensor_tensor(x, x, lngb[:, 512:1024], ALU.add).then_inc(S("ln_rows"), 1)
            def score_rows(n):
                tile = 1 - n % 2
                w = NG * (T if tile else P)
                mo = 0 if tile else NG * T
                c = 100 + 4 * (n % 2)
                dve.wait_ge(S("scores"), n + 1)
                for lo in range(0, w, 512):
                    m = min(512, w - lo)
                    last = v.tensor_tensor(sc[n % 2][:, lo:lo + m], bank[4 + 2 * (n % 2) + lo // 512][:, 0:m],
                                           amask[:, mo + lo:mo + lo + m], ALU.add)
                link(last)
                link(v.tensor_reduce(stat[:, c + 2:c + 3], sc[n % 2][:, 0:w], AX_X, ALU.max))
                v.tensor_scalar(stat[:, c:c + 1], stat[:, c + 2:c + 3], -(HD ** -0.5), None, ALU.mult) \
                    .then_inc(S("scored"), 1)

            score_rows(0)
            for n in range(2 * AH):
                hd, tile = n // 2, 1 - n % 2
                c = 100 + 4 * (n % 2)
                dve.wait_ge(S("probs_turned"), n + 1)
                if tile:
                    dve.wait_ge(S("PT_half"), n // 2 + 1)
                    v.tensor_copy(PTb[:, 512:768], bank[3][:, 0:256]).then_inc(S("PT_ready"), 1)
                if n + 1 < 2 * AH:
                    score_rows(n + 1)
                link(v.reciprocal(stat[:, c + 3:c + 4], stat[:, c + 1:c + 2]))
                dve.wait_ge(S("pv"), n + 1)
                v.tensor_scalar(attn[:, tile, hd * HD:(hd + 1) * HD], bank[4 + 2 * (n % 2)][:, 0:HD],
                                stat[:, c + 3:c + 4], None, ALU.mult).then_inc(S("attn_rows"), 1)
            for t in range(NT):
                dve.wait_ge(S("attn_turned"), t + 1)
                v.tensor_copy(aT[:, :, t * P:(t + 1) * P], bank[6 + t][:, :].rearrange("p (c t) -> p c t", c=4)) \
                    .then_inc(S("aT_ready"), 1)
            for t in range(NT):
                dve.wait_ge(S("mixed"), 2)
                x = uv[:, t, 512:1024].rearrange("p (g c) -> p g c", g=SG)
                link(v.tensor_tensor(x, bank[4 + t][:, :].rearrange("p (g c) -> p g c", g=SG),
                                     V("b_spatial_2", 0, 8).unsqueeze(2).to_broadcast([P, SG, HD]), ALU.add))
                v.tensor_tensor(uv[:, t, 0:512], uv[:, t, 0:512], uv[:, t, 512:1024], ALU.mult).then_inc(S("sgu_rows"), 1)
            for t in range(NT):
                dve.wait_ge(S("sgu_turned"), t + 1)
                v.tensor_copy(sT[:, :, t * P:(t + 1) * P], bank[6 + t][:, :].rearrange("p (c t) -> p c t", c=4)) \
                    .then_inc(S("sT_ready"), 1)
            dve.wait_ge(S("evac"), 47 + 22 + 16)
            merge("proj_a", "proj_b", "merged2", gate[:, 0:KC, :], gate[:, KC:2 * KC, :], mT2, scw)
            dve.wait_ge(S("out_merged2"), 2)
            add_rows("out_merged2", "x3_added")
            norm_rows("n4", ((0, P), (1, P)), h, xn2, 64)
            turned_out("n4", ((0, P), (P, P)), hn2, "norm2_g_2")
            for c in range(FC):
                dve.wait_ge(S("ff_silu"), c + 1)
                v.tensor_tensor(ffT[:, c, :], sgf[:, c % 4, :], bank[4 + c % 4][:, T:2 * T], ALU.mult) \
                    .then_inc(S("ff_cols"), 1)
            dve.wait_ge(S("out_ff_cols"), 6)
            add_rows("out_ff_cols", "x4_added")
            dve.wait_ge(S("fg2_loaded"), 16)
            for t in range(NT):
                dve.wait_ge(S("norm_rstd"), STATS["f2"] + t + 1)
                v.scalar_tensor_tensor(out=outr[:, t, :], in0=h[:, t, :], scalar=stat[:, 104 + t:105 + t], in1=fgb2,
                                       op0=ALU.mult, op1=ALU.mult).then_inc(S("out_rows"), 1)


_INS = ["x", "meta_tokens", "norm1_g", "w_in", "hg_lower_bounds", "hg_norm_g", "conv_w", "conv_b", "lru_w_r",
        "lru_b_r", "lru_w_i", "lru_b_i", "lru_lambda", "w_up_a", "w_up_b", "w_out", "norm2_g", "w_group",
        "b_group", "w_router", "b_router", "w_gate", "w_up", "w_down", "final_g", "positions_2", "norm1_g_2",
        "w_in_2", "sgu_ln_g_2", "sgu_ln_b_2", "w_spatial_2", "b_spatial_2", "w_proj_attn_2", "w_proj_sgu_2",
        "w_out_2", "norm2_g_2", "w_ffn_gate_2", "w_ffn_up_2", "w_ffn_down_2", "final_g_2"]


def kernel(**inputs):
    import numpy as _np
    import concourse.bacc as _bacc
    from concourse import mybir as _mybir
    from concourse.bass_utils import run_bass_kernel_spmd as _run

    nc = _bacc.Bacc("TRN2", target_bir_lowering=False, num_devices=1)
    arrays, aps = {}, {}
    for name in _INS:
        a = _np.ascontiguousarray(inputs[name])
        arrays[f"in_{name}"] = a
        aps[name] = nc.dram_tensor(f"in_{name}", a.shape, _mybir.dt.from_np(a.dtype), kind="ExternalInput").ap()
    out = nc.dram_tensor("out_0", (1, T, D), _mybir.dt.float32, kind="ExternalOutput").ap()
    build(nc, aps, out)
    r = _run(nc, [arrays], core_ids=[0])
    return r.results[0]["out_0"]
```

```python
from contextlib import ExitStack

import numpy as np
import concourse.bass as bass
from concourse import mybir

ALU = mybir.AluOpType
ACT = mybir.ActivationFunctionType
F32 = mybir.dt.float32
I32 = mybir.dt.int32
AX_X = mybir.AxisListType.X

P = 128
D = 1024
KC = D // P
T = 256
NT = T // P
META = 16
TT = META + T
EPS = 1e-6
HEADS = 4
NE = 32
GROUPS = 4
EPG = NE // GROUPS
CAP = 64
PAIRS = NE // 2
PASSES = T // CAP
SLOTS = NE * CAP
DE = 512
FF = 2816
FC = FF // P
RING = 6
UW = 4096
AH = 8
NG = 3
HD = 64
SG = 8
NEG = -1.0e30
INV_FREQ = [float(np.float32(500000.0 ** (-j / 16.0))) for j in range(0, 16, 2)]
LEVELS = [64, 32, 16, 8, 4, 2, 1]

VEC_ROWS = [("norm1_g", 8), ("hg_lower_bounds", 8), ("hg_norm_g", 4), ("conv_w", 32), ("conv_b", 8),
            ("lru_b_r", 8), ("lru_b_i", 8), ("lru_lambda", 8), ("norm1_g_2", 8), ("norm2_g_2", 8),
            ("b_spatial_2", 8)]
VEC_AT = {}
NVR = 0
for _name, _n in VEC_ROWS:
    VEC_AT[_name] = NVR
    NVR += _n

B1_UNITS = ["i", "f", "q", "lx0", "lx1", "ly0", "ly1", "og", "ga0", "ga1", "lru", "gb0", "gb1",
            "up_a", "up_b0", "up_b1", "out0", "out1"]
MOE_UNITS = ["g0", "g1", "u0", "u1", "d0", "d1"]
B2_UNITS = (["q0", "q1", "q2", "k0", "k1", "k2", "v0", "v1", "v2", "uv0", "uv1", "ga0", "ga1", "gb0", "gb1",
             "pa", "ps", "out0", "out1"] + [f"ff{n}" for n in range(11)] + [f"fd{n}" for n in range(6)])
MOE0 = len(B1_UNITS)
LAST0 = MOE0 + 6 * (PAIRS - 1)
B2_0 = LAST0 + 2
assert MOE0 % RING == 0
B1_OUTS = 47
W1_COL = {"q": 0, "f": 512, "i": 1024, "og": 1536, "lx0": 2048, "lx1": 2560, "ly0": 3072, "ly1": 3584,
          "ga0": 4096, "ga1": 4608, "gb0": 5120, "gb1": 5632}


STATS = {"n1": 0, "n2": 3, "f1": 5, "n3": 7, "ln": 9, "n4": 11, "f2": 13}
ROWS = {"n1": 0, "n2": 3, "n3": 5, "n4": 7}


def transfers(name, block):
    return 2 if (name == "lru" or (block == 2 and name.startswith("ff"))) else 1


def landed_values():
    total = [0] * RING
    value = {}
    for u in range(B2_0 + len(B2_UNITS)):
        if u < MOE0:
            n = transfers(B1_UNITS[u], 1)
        elif u < B2_0:
            n = 1
        else:
            n = transfers(B2_UNITS[u - B2_0], 2)
        total[u % RING] += 16 * n
        value[u] = total[u % RING]
    return value


LANDED = landed_values()


def used(u):
    if u < MOE0:
        name = B1_UNITS[u]
        if name == "lru":
            return "lru_products", 2 * KC
        if name.startswith("up"):
            return ("up_a", 1) if name == "up_a" else ("up_b", KC)
        if name.startswith("out"):
            return "out_merged", NT
        return "projected", 3 + 4 * (u if u < 10 else u - 1)
    if u < B2_0:
        if u >= LAST0:
            return "y_ready", PAIRS
        assert u >= LAST0 - 6
        return ("gates", "ups", "y_ready")[(u - MOE0) % 6 // 2], PAIRS - 1
    n = u - B2_0
    if n < 11:
        return "projected", B1_OUTS + 2 * (n + 1)
    if n < 15:
        return "projected", B1_OUTS + 22 + 4 * (n - 10)
    if n < 17:
        return ("proj_a", 1) if n == 15 else ("proj_b", KC)
    if n < 19:
        return "out_merged2", NT
    if n < 30:
        return "ff", 2 * (n - 18)
    return "out_ff_cols", NT


def build(nc, A, out):
    ctx = ExitStack()
    with ctx:
        def sb(name, shape, dt=F32):
            return ctx.enter_context(nc.sbuf_tensor(name, shape, dt))

        sems = {}

        def S(name):
            if name not in sems:
                sems[name] = ctx.enter_context(nc.semaphore(name))
            return sems[name]

        bank = [ctx.enter_context(nc.psum_tensor(f"bank{b}", [P, 512], F32)) for b in range(8)]
        ring = sb("ring", [P, RING, UW])
        ident = sb("ident", [P, P])
        ones = sb("ones", [P, P])
        h = sb("h", [P, NT, D])
        vec = sb("vec", [P, NVR])
        cst = sb("cst", [P, 64])
        stat = sb("stat", [P, 128])
        route = sb("route", [P, 1400])
        idx = sb("idx", [P, 64], I32)
        arena_words = 24552
        arena = sb("arena", [P, arena_words])
        top = {}

        def at(region, words):
            o = top[region]
            top[region] = o + words
            assert o + words <= arena_words, (region, o + words)
            return arena[:, o:o + words]

        hf_d = nc.dram_tensor("hf_rows", [T, D], F32).ap()

        top["m1"] = 0
        wz = at("m1", 3072)
        xn = wz.rearrange("p (t d) -> p t d", t=3)
        hnT = at("m1", KC * TT).rearrange("p (c t) -> p c t", c=KC)
        v1 = at("m1", 1536).rearrange("p (t d) -> p t d", t=3)
        fkg0 = top["m1"]
        sf = at("m1", HEADS * TT).rearrange("p (c t) -> p c t", c=HEADS)
        kk = at("m1", HEADS * TT).rearrange("p (c t) -> p c t", c=HEADS)
        kx = at("m1", HEADS * T).rearrange("p (c t) -> p c t", c=HEADS)
        Gx = at("m1", HEADS * T).rearrange("p (c t) -> p c t", c=HEADS)
        Gm = at("m1", HEADS * META).rearrange("p (c t) -> p c t", c=HEADS)
        lx = at("m1", KC * (3 + TT)).rearrange("p (c t) -> p c t", c=KC)
        ly = at("m1", KC * T).rearrange("p (c t) -> p c t", c=KC)
        og = at("m1", HEADS * T).rearrange("p (c t) -> p c t", c=HEADS)
        ga = at("m1", KC * T).rearrange("p (c t) -> p c t", c=KC)
        zo = top["m1"]
        qx = at("m1", HEADS * T).rearrange("p (c t) -> p c t", c=HEADS)
        z1 = at("m1", HEADS * T)
        PT = at("m1", 1024).rearrange("p (c t) -> p c t", c=8)
        St = at("m1", 1024).rearrange("p (k h v) -> p k h v", k=2, h=HEADS)
        kT = z1.rearrange("p (k n) -> p k n", k=2)
        meta = z1
        maskw = at("m1", 8 * P).bitcast(I32).rearrange("p (l t) -> p l t", l=8)
        oT = at("m1", HEADS * T).rearrange("p (c t) -> p c t", c=HEADS)
        m1_end = top["m1"]
        vecrows = oT.rearrange("p c t -> p (c t)")[:, 0:P]
        W = [wz[:, 0:1024], wz[:, 1024:2048]]
        z = [wz[:, 2048:3072], z1]
        kE = wz[:, 2048:3072]
        top["xc"] = fkg0
        xc = at("xc", KC * TT).rearrange("p (c t) -> p c t", c=KC)
        assert top["xc"] <= fkg0 + 2 * HEADS * TT
        lrur = lx[:, :, 0:TT]
        o0 = 0
        lrui = arena[:, o0:o0 + KC * TT].rearrange("p (c t) -> p c t", c=KC)
        lrua = arena[:, zo:zo + KC * TT].rearrange("p (c t) -> p c t", c=KC)
        lrut = arena[:, zo + KC * TT:zo + 2 * KC * TT].rearrange("p (c t) -> p c t", c=KC)
        assert zo + 2 * KC * TT <= m1_end - HEADS * T
        rsn = v1[:, 0:2, :].rearrange("p t d -> p (t d)")
        gb = arena[:, fkg0 + 2 * HEADS * TT:fkg0 + 2 * HEADS * TT + KC * T].rearrange("p (c t) -> p c t", c=KC)
        mT = hnT[:, :, 0:T]

        top["moe"] = 0
        hf = at("moe", NT * D).rearrange("p (t d) -> p t d", t=NT)
        hfT = at("moe", KC * T).rearrange("p (c t) -> p c t", c=KC)
        fgb = at("moe", D)
        at("moe", P)
        g2b = at("moe", D)
        assert top["moe"] <= 3072 + KC * TT + 1536 and top["moe"] - D >= 3072 + KC * TT
        xg = at("moe", D)
        xgT = at("moe", KC * 2 * CAP).rearrange("p (c t) -> p c t", c=KC)
        sg = at("moe", DE)
        hid = at("moe", DE)
        hT = at("moe", 4 * 2 * CAP).rearrange("p (k n) -> p k n", k=4)
        ysb = at("moe", D)
        side_u0 = at("moe", UW)
        sw = at("moe", NT * 2 * CAP).rearrange("p (t e s) -> p t e s", t=NT, e=2)
        swT = at("moe", NT * P).rearrange("p (t n) -> p t n", t=NT)
        lists = at("moe", PASSES * PAIRS).bitcast(I32)
        slot_hot = at("moe", 4 * 2 * CAP).rearrange("p (k n) -> p k n", k=4)
        list_hot = at("moe", 4 * PASSES * PAIRS).rearrange("p (k n) -> p k n", k=4)
        side = [arena[:, arena_words - 2 * UW:arena_words - UW], arena[:, arena_words - UW:arena_words],
                side_u0, arena[:, 0:UW]]
        assert top["moe"] <= arena_words - 2 * UW and NT * D + KC * T == UW

        top["b2"] = 0
        xn2 = at("b2", NT * D).rearrange("p (t d) -> p t d", t=NT)
        hn2 = at("b2", KC * T).rearrange("p (c t) -> p c t", c=KC)
        top["x2"] = 0
        qk = [xn2[:, :, 0:512], xn2[:, :, 512:1024]]
        qkT = at("b2", 24 * T).rearrange("p (c t) -> p c t", c=24)
        vv = at("b2", NT * NG * 512).rearrange("p (t d) -> p t d", t=NT)
        uv = at("b2", NT * D).rearrange("p (t d) -> p t d", t=NT)
        gate = at("b2", 2 * KC * T).rearrange("p (c t) -> p c t", c=2 * KC)
        amask = at("b2", 1152)
        ffo = top["b2"]
        scw = at("b2", 1536)
        sc = [scw[:, 0:768], scw[:, 768:1536]]
        aT = at("b2", 4 * T).rearrange("p (c t) -> p c t", c=4)
        rtmp = scw[:, 1024:1536].rearrange("p (k n) -> p k n", k=4)
        wsT = xn2[:, 0, :].rearrange("p (g t) -> p g t", g=SG)
        lngb = xn2[:, 1, :]
        PTb = at("b2", 768)
        sT = xn2[:, 1, :].rearrange("p (c t) -> p c t", c=4)
        wsr = aT.rearrange("p c t -> p (c t)")
        mT2 = hn2
        ffT = qkT.rearrange("p c t -> p (c t)")[:, 0:FC * T].rearrange("p (c t) -> p c t", c=FC)
        sgf = scw[:, 0:1024].rearrange("p (k t) -> p k t", k=4)
        fgb2 = gate.rearrange("p c t -> p (c t)")[:, 0:D]
        outr = gate.rearrange("p c t -> p (c t)")[:, D:3 * D].rearrange("p (t d) -> p t d", t=NT)

        def not_zero(eng, name, value):
            if not (isinstance(value, int) and value == 0):
                eng.wait_ge(S(name), value)

        def V(name, k=0, n=1):
            return vec[:, VEC_AT[name] + k:VEC_AT[name] + k + n]

        def bc(ap, shape, axis):
            return ap.unsqueeze(axis).to_broadcast(shape)

        negh = cst[:, 0:1]
        lbv = cst[:, 4:8]
        omlb = cst[:, 8:12]
        sp8 = cst[:, 12:20]
        tmp8 = cst[:, 20:28]
        m2sp = cst[:, 28:36]
        egA = cst[:, 36:40]
        pdt = cst[:, 40:48]

        def w3(u, k):
            return ring[:, u % RING, :].rearrange("p (k n) -> p k n", k=k)

        bias36 = route[:, 0:36]
        lg = route[:, 40:112].rearrange("p (t e) -> p t e", t=2)
        iota32 = route[:, 112:144]
        half_of = route[:, 144:176]
        pair_of = route[:, 176:208]
        tokid = route[:, 208:210]
        ustr = route[:, 210:338]
        rt = route[:, 340:984]
        iota128 = route[:, 984:1112]
        rw = route[:, 1112:1400].rearrange("p (c e) -> p c e", c=KC)
        block = ctx.enter_context(nc.Block())

        @block.sync
        def _(sp):
            w1 = A["w_in"][0].rearrange("(k p) n -> p k n", p=P)
            w2 = A["w_in_2"][0].rearrange("(k p) n -> p k n", p=P)

            def slot_free(u):
                if u >= RING:
                    name, value = used(u - RING)
                    sp.wait_ge(S(name), value)

            def load(u, src, dst=None):
                dst = ring[:, u % RING, :] if dst is None else dst
                sp.dma_start(dst, src).then_inc(S(f"landed{u % RING}"), 16)

            sp.wait_ge(S("params_issued"), 1)
            for u, name in enumerate(B1_UNITS):
                slot_free(u)
                if name in W1_COL:
                    load(u, w1[:, :, W1_COL[name]:W1_COL[name] + 512], w3(u, KC))
                elif name == "lru":
                    load(u, A["lru_w_r"][0].rearrange("n i j -> i n j"), w3(u, 32)[:, 0:8, :])
                    load(u, A["lru_w_i"][0].rearrange("n i j -> i n j"), w3(u, 32)[:, 8:16, :])
                elif name == "up_a":
                    load(u, A["w_up_a"][0].rearrange("(k p) n -> p k n", p=P), w3(u, 4))
                else:
                    src = A["w_up_b"] if name.startswith("up_b") else A["w_out"]
                    load(u, src[0].rearrange("(k p) n -> p k n", p=P)[:, 4 * int(name[-1]):4 * int(name[-1]) + 4, :],
                         w3(u, 4))

            gate_w = A["w_gate"][0].rearrange("e (k p) n -> e p k n", p=P)
            up_w = A["w_up"][0].rearrange("e (k p) n -> e p k n", p=P)
            down_w = A["w_down"][0].rearrange("e (k p) n -> e p k n", p=P)

            def expert_unit(j, e2):
                src = {"g": gate_w, "u": up_w, "d": down_w}[MOE_UNITS[j][0]]
                return src[bass.ds(e2 + int(MOE_UNITS[j][1]), 1)].rearrange("e p k n -> p e k n")

            def expert_dst(j):
                return w3(j, KC if MOE_UNITS[j][0] != "d" else 4).unsqueeze(1)

            for j in range(6):
                slot_free(MOE0 + j)
                sp.dma_start(expert_dst(j), expert_unit(j, 0)).then_inc(S(f"landed{j}"), 16)
            for j in range(4):
                if j == 0:
                    sp.wait_ge(S("out_merged"), 2)
                elif j == 2:
                    sp.wait_ge(S("hf_stored"), 16 * NT)
                    sp.wait_ge(S("logits"), NT)
                    sp.wait_ge(S("rows_in"), 16)
                sp.dma_start(side[j].rearrange("p (k n) -> p k n", k=KC).unsqueeze(1), expert_unit(j, NE - 2)) \
                    .then_inc(S("side_gates" if j < 2 else "side_ups"), 16)
            with sp.Fori(1, PAIRS - 1) as i:
                for j in range(6):
                    sp.wait_ge(S(("gates", "ups", "y_ready")[j // 2]), i)
                    sp.dma_start(expert_dst(j), expert_unit(j, 2 * i)).then_inc(S(f"landed{j}"), 16)

            for e in range(2):
                slot_free(LAST0 + e)
                load(LAST0 + e, expert_unit(4 + e, NE - 2), w3(LAST0 + e, 4).unsqueeze(1))

            sp.wait_ge(S("flag_set"), 1)
            over = sp.value_load(idx[0:1, 40:41], min_val=0, max_val=T)
            with sp.If(over > CAP):
                sp.wait_ge(S("y_ready"), PAIRS)
                with sp.Fori(0, PASSES - 1) as a:
                    with sp.Fori(0, PAIRS) as i:
                        for j in range(6):
                            sp.wait_ge(S("over_y"), PAIRS * a + i + 1)
                            sp.dma_start(expert_dst(j), expert_unit(j, 2 * i)).then_inc(S("over_landed"), 16)
                sp.wait_ge(S("over_y"), (PASSES - 1) * PAIRS + 1)

            for n, name in enumerate(B2_UNITS):
                u = B2_0 + n
                slot_free(u)
                if n < 15:
                    load(u, w2[:, :, 512 * n:512 * n + 512], w3(u, KC))
                elif name in ("pa", "ps"):
                    src = A["w_proj_attn_2"] if name == "pa" else A["w_proj_sgu_2"]
                    load(u, src[0].rearrange("(k p) n -> p k n", p=P), w3(u, 4))
                elif name.startswith("out"):
                    c = 4 * int(name[-1])
                    load(u, A["w_out_2"][0].rearrange("(k p) n -> p k n", p=P)[:, c:c + 4, :], w3(u, 4))
                elif name.startswith("ff"):
                    c = 256 * int(name[2:])
                    for q, key in enumerate(("w_ffn_gate_2", "w_ffn_up_2")):
                        load(u, A[key][0].rearrange("(k p) n -> p k n", p=P)[:, :, c:c + 256],
                             w3(u, 2 * KC)[:, KC * q:KC * q + KC, :])
                else:
                    c = 4 * int(name[2:])
                    m = min(4, FC - c)
                    load(u, A["w_ffn_down_2"][0].rearrange("(k p) n -> p k n", p=P)[:, c:c + m, :],
                         w3(u, 4)[:, 0:m, :])
            for t in range(NT):
                sp.wait_ge(S("out_rows"), t + 1)
                sp.dma_start(out[0, t * P:(t + 1) * P, :], outr[:, t, :]).then_inc(S("stored"), 16)
            sp.wait_ge(S("stored"), 16 * NT)

        @block.gpsimd
        def _(pool):
            n_link = [0]

            def link(ins):
                n_link[0] += 1
                ins.then_inc(S("pool_chain"), 1)
                pool.wait_ge(S("pool_chain"), n_link[0])

            link(pool.memset(ident[:, :], 0.0))
            link(pool.memset(ones[:, :], 1.0))
            link(pool.affine_select(out=ident[:, :], in_=ident[:, :], compare_op=ALU.not_equal, fill=1.0,
                                    base=0, pattern=[[-1, P]], channel_multiplier=1))
            link(pool.memset(negh, -0.5))
            link(pool.memset(lx[:, :, 0:3], 0.0))
            pool.iota(idx[:, 60:61], [[0, 1]], base=0, channel_multiplier=1).then_inc(S("iotas"), 1)
            pool.iota(maskw[:, 7, :], [[1, P]], base=0, channel_multiplier=0).then_inc(S("iotas"), 1)

            def power(name, n, count, parts, scale):
                pool.wait_ge(S("norm_sums"), STATS[name] + count)
                link(pool.tensor_scalar(stat[0:parts, n + 8:n + 9], stat[0:parts, n:n + 1], scale, EPS,
                                        ALU.mult, ALU.add))
                pool.tensor_tensor(stat[0:parts, n + 16:n + 17], stat[0:parts, n + 8:n + 9],
                                   negh[0:parts, :], ALU.pow).then_inc(S("norm_rstd"), 1)

            for j, (parts, tile) in enumerate(((META, 2), (P, 0), (P, 1))):
                power("n1", tile, j + 1, parts, 1.0 / D)

            link(pool.memset(ustr, 1.0))
            link(pool.affine_select(out=ustr, in_=ustr, compare_op=ALU.is_gt, fill=0.0,
                                    base=0, pattern=[[1, P]], channel_multiplier=-1))
            pool.iota(iota32, [[1, 32]], base=0, channel_multiplier=0,
                      allow_small_or_imprecise_dtypes=True).then_inc(S("route_consts"), 1)
            pool.iota(half_of, [[0, PAIRS], [CAP, 2]], base=0, channel_multiplier=0,
                      allow_small_or_imprecise_dtypes=True).then_inc(S("route_consts"), 1)
            pool.iota(pair_of, [[1, PAIRS], [0, 2]], base=0, channel_multiplier=0,
                      allow_small_or_imprecise_dtypes=True).then_inc(S("route_consts"), 1)
            pool.iota(tokid, [[P, 2]], base=0, channel_multiplier=1,
                      allow_small_or_imprecise_dtypes=True).then_inc(S("route_consts"), 1)
            pool.iota(iota128, [[1, P]], base=0, channel_multiplier=0,
                      allow_small_or_imprecise_dtypes=True).then_inc(S("route_consts"), 1)

            for t in range(NT):
                power("n2", 24 + t, t + 1, P, 1.0 / D)

            pool.wait_ge(S("lists_set"), 1)
            pool.wait_ge(S("hf_stored"), 32)

            def gather(dst, src, column):
                return pool.indirect_dma_start(dst, None, src,
                                               bass.IndirectOffsetOnAxis(ap=column, axis=0))

            gather(xg[:, :], hf_d, lists[:, 0:1]).then_inc(S("rows_in"), 16)
            for i in range(1, PAIRS):
                pool.wait_ge(S("rows_turned"), i)
                gather(xg[:, :], hf_d, lists[:, i:i + 1]).then_inc(S("rows_in"), 16)

            pool.wait_ge(S("flag_set"), 1)
            over = pool.value_load(idx[0:1, 40:41], min_val=0, max_val=T)
            with pool.If(over > CAP):
                pool.wait_ge(S("rows_turned"), PAIRS)
                for n in range((PASSES - 1) * PAIRS):
                    gather(xg[:, :], hf_d, lists[:, PAIRS + n:PAIRS + n + 1]).then_inc(S("over_rows"), 16)
                    pool.wait_ge(S("over_y"), n + 2)

            for t in range(NT):
                power("f1", 48 + t, t + 1, P, 1.0 / D)
            for t in range(NT):
                power("n3", 50 + t, t + 1, P, 1.0 / D)

            def keep(view, base, pattern, cm, op):
                link(pool.affine_select(out=view, in_=view, compare_op=op, fill=NEG, base=base,
                                        pattern=pattern, channel_multiplier=cm))

            pool.wait_ge(S("x2_ready"), NT)
            link(pool.memset(amask, 0.0))
            for g, dil in enumerate((1, 4, 16)):
                for tile, o, n in ((1, T * g, T), (0, NG * T + P * g, P)):
                    view = amask[:, o:o + n]
                    keep(view, P * tile, [[-1, n]], 1, ALU.is_ge)
                    if g == 0:
                        keep(view, P - P * tile, [[1, n]], -1, ALU.is_ge)
            pool.iota(scw[:, 0:T].bitcast(I32), [[-1, T]], base=P + 0, channel_multiplier=1) \
                .then_inc(S("diff_iota"), 1)
            pool.wait_ge(S("ws_loaded"), 16)
            ws3 = wsr.rearrange("p (g s) -> p g s", g=SG)
            pool.affine_select(out=ws3, in_=ws3, compare_op=ALU.is_ge, fill=0.0, base=0,
                               pattern=[[0, SG], [-1, P]], channel_multiplier=1).then_inc(S("ws_masked"), 1)

            for t in range(NT):
                power("ln", 56 + t, t + 1, P, 1.0)
            for t in range(NT):
                power("n4", 64 + 0 + t, t + 1, P, 1.0 / D)
            for t in range(NT):
                power("f2", 88 + t, t + 1, P, 1.0 / D)

        @block.tensor
        def _(pe):
            mm = nc.tensor.matmul
            tr = nc.tensor.transpose

            def take(u):
                pe.wait_ge(S(f"landed{u % RING}"), LANDED[u])

            def turn_rows(rows, name, src, n_tiles):
                for j in range(n_tiles):
                    tile, n = rows[j]
                    pe.wait_ge(S("norm_rows"), ROWS[name] + j + 1)
                    for half in range(2):
                        for c in range(4):
                            k = 4 * half + c
                            last = tr(bank[2 * j + half][:, c * n:(c + 1) * n], src[0:n, tile, k * P:(k + 1) * P],
                                      ident[0:n, 0:n])
                        last.then_inc(S("norm_turned"), 1)

            pe.wait_ge(S("pool_chain"), 3)
            pe.wait_ge(S("vec_loaded"), 16 * len(VEC_ROWS))
            tr(bank[7][:, 0:NVR], vecrows[0:NVR, :], ident[0:NVR, 0:NVR]).then_inc(S("vec_turned"), 1)
            turn_rows(((2, META), (0, P), (1, P)), "n1", xn, 3)

            n_out = [0]

            def out_bank():
                n = n_out[0]
                n_out[0] += 1
                if n >= 4:
                    pe.wait_ge(S("evac"), n - 3)
                return bank[n % 4]

            def project_cols(u, first, hn, lo, n):
                take(u)
                for m in range(4):
                    b = out_bank()
                    for k in range(KC):
                        last = mm(b[:, 0:n], w3(u, KC)[:, k, m * P:(m + 1) * P], hn[:, k, lo:lo + n],
                                  start=(k == 0), stop=(k == KC - 1))
                    last.then_inc(S("projected"), 1)

            def project_rows(u, tiles, hn):
                take(u)
                for lo, n in tiles:
                    b = out_bank()
                    for k in range(KC):
                        last = mm(b[0:n, :], hn[:, k, lo:lo + n], w3(u, KC)[:, k, :],
                                  start=(k == 0), stop=(k == KC - 1))
                    last.then_inc(S("projected"), 1)

            pe.wait_ge(S("norm_done"), 2 * ROWS["n1"] + 6)
            project_rows(0, ((0, META), (META, P), (META + P, P)), hnT)
            project_cols(1, 0, hnT, 0, TT)
            project_cols(2, 0, hnT, META, T)
            project_cols(3, 0, hnT, 0, TT)

            for part in range(2):
                n = (META, P)[part]
                pe.wait_ge(S("k_end"), part + 1)
                for hd in range(HEADS):
                    last = tr(bank[4][0:n, hd * P:(hd + 1) * P],
                              kE[:, hd * P:hd * P + n], ident[:, :])
                last.then_inc(S("k_turned"), 1)
                pe.wait_ge(S("kT_ready"), part + 1)
                for hd in range(HEADS):
                    last = mm(bank[5][:, hd * P:(hd + 1) * P], kT[0:n, part, hd * P:(hd + 1) * P],
                              v1[0:n, (2, 0)[part], hd * P:(hd + 1) * P], start=True, stop=True)
                last.then_inc(S("kv"), 1)
                if part == 0:
                    pe.wait_ge(S("state"), 1)
            pe.wait_ge(S("state"), 2)

            def level(l):
                if l < 7:
                    pe.wait_ge(S("z_ready"), l + 1)
                if l >= 2:
                    pe.wait_ge(S("picked"), l - 1)
                for c in range(8):
                    lo = (c // 2) * T + (c % 2) * P
                    if l < 7:
                        a = b = z[l % 2][:, lo:lo + P]
                    else:
                        a = kx.rearrange("p c t -> p (c t)")[:, lo:lo + P]
                        b = qx.rearrange("p c t -> p (c t)")[:, lo:lo + P]
                    last = mm(bank[4 + 2 * (l % 2) + c // 4][:, (c % 4) * P:(c % 4 + 1) * P], a, b,
                              start=True, stop=True)
                last.then_inc(S("levels"), 1)

            project_cols(4, 0, hnT, 0, TT)
            level(0)
            level(1)
            project_cols(5, 0, hnT, META, T)
            level(2)
            level(3)
            project_cols(6, 0, hnT, META, T)
            level(4)
            level(5)
            project_cols(7, 0, hnT, META, T)
            level(6)
            level(7)
            project_cols(8, 0, hnT, META, T)
            pe.wait_ge(S("picked"), 8)
            pe.wait_ge(S("qe_ready"), 1)
            for hd in range(HEADS):
                for c in range(2):
                    o = bank[4 + hd // 2][:, (hd % 2) * T + c * P:(hd % 2) * T + (c + 1) * P]
                    mm(o, v1[:, c, hd * P:(hd + 1) * P], PT[:, 2 * hd + c, :], start=True, stop=False)
                    last = mm(o, St[:, c, hd, :], qx[:, hd, c * P:(c + 1) * P], start=False, stop=True)
            last.then_inc(S("o_ready"), 1)
            project_cols(9, 0, hnT, META, T)
            pe.wait_ge(S("o_squared"), 2)
            for c in range(2):
                last = mm(bank[6 + c][:, :], ones[:, :], W[0][:, c * 512:(c + 1) * 512], start=True, stop=True)
            last.then_inc(S("o_sums"), 1)
            take(10)
            pe.wait_ge(S("o_mean"), 1)
            for b in range(KC):
                for q in range(2):
                    n = 2 * b + q
                    if b == 0:
                        pe.wait_ge(S("conv"), KC)
                    if n >= 4:
                        pe.wait_ge(S("lru_gates"), n - 3)
                    last = mm(bank[4 + n % 4][:, 0:TT], w3(10, 32)[:, 8 * q + b, :], xc[:, b, :],
                              start=True, stop=True)
                    last.then_inc(S("lru_products"), 1)
            project_cols(11, 0, hnT, META, T)
            project_cols(12, 0, hnT, META, T)
            pe.wait_ge(S("evac"), n_out[0])
            pe.wait_ge(S("oa_ready"), 1)
            take(13)
            for m in range(KC):
                for k in range(HEADS):
                    last = mm(bank[m // 2][:, (m % 2) * T:(m % 2 + 1) * T], w3(13, 4)[:, k, m * P:(m + 1) * P],
                              oT[:, k, :], start=(k == 0), stop=(k == HEADS - 1))
            last.then_inc(S("up_a"), 1)
            pe.wait_ge(S("lru_gates"), 16)
            pe.wait_ge(S("ob_ready"), 1)
            take(14)
            take(15)
            for m in range(KC):
                for k in range(KC):
                    last = mm(bank[4 + m // 2][:, (m % 2) * T:(m % 2 + 1) * T],
                              w3(14 + k // 4, 4)[:, k % 4, m * P:(m + 1) * P],
                              ly[:, k, :], start=(k == 0), stop=(k == KC - 1))
                last.then_inc(S("up_b"), 1)

            def out_projection(u0, src, ready, n_units, total):
                for t in range(NT):
                    for k in range(total):
                        if t == 0 and k % 4 == 0:
                            take(u0 + k // 4)
                        if t == 0 and k == 0:
                            pe.wait_ge(S(ready), total)
                        for half in range(2):
                            last = mm(bank[2 * t + half][:, :], src[:, k, t * P:(t + 1) * P],
                                      w3(u0 + k // 4, 4)[:, k % 4, half * 512:(half + 1) * 512],
                                      start=(k == 0), stop=(k == total - 1))
                    last.then_inc(S("out_" + ready), 1)

            out_projection(16, mT, "merged", 2, KC)

            turn_rows(((0, P), (1, P)), "n2", hf, 2)
            pe.wait_ge(S("norm_done"), 2 * ROWS["n2"] + 4)
            pe.wait_ge(S("rw_loaded"), 16 * 5)
            for t in range(NT):
                for k in range(KC):
                    last = mm(bank[4 + t][:, 0:36], hfT[:, k, t * P:(t + 1) * P], rw[:, k, :],
                              start=(k == 0), stop=(k == KC - 1))
                last.then_inc(S("logits"), 1)
            pe.wait_ge(S("chosen"), 1)
            M = rt[:, 0:64]
            mm(bank[6][:, 0:32], ustr, M[:, 0:32], start=True, stop=True)
            mm(bank[6][:, 32:64], ones[:, :], M[:, 0:32], start=True, stop=False)
            mm(bank[6][:, 32:64], ustr, M[:, 32:64], start=False, stop=True)
            mm(bank[6][:, 64:96], ones[:, :], M[:, 0:32], start=True, stop=False)
            mm(bank[6][:, 64:96], ones[:, :], M[:, 32:64], start=False, stop=True).then_inc(S("places"), 1)

            pe.wait_ge(S("slot_hot"), 1)
            pe.wait_ge(S("list_hot"), 1)
            for q in range(4):
                last = mm(bank[7][:, 0:PASSES * PAIRS], slot_hot[:, q, :], list_hot[:, q, :],
                          start=(q == 0), stop=(q == 3))
            last.then_inc(S("lists"), 1)

            def turn_pair():
                for k in range(KC):
                    last = tr(bank[2 + k // 4][:, (k % 4) * 2 * CAP:(k % 4 + 1) * 2 * CAP],
                              xg[:, k * P:(k + 1) * P], ident[:, :])
                return last

            def products(b, weights):
                for k in range(KC):
                    for e in range(2):
                        last = mm(bank[b][e * CAP:(e + 1) * CAP, :], xgT[:, k, e * CAP:(e + 1) * CAP],
                                  weights[e][:, k, :], start=(k == 0), stop=(k == KC - 1))
                return last

            def turn_hidden():
                for k in range(4):
                    last = tr(bank[0][:, k * P:(k + 1) * P], hid[:, k * P:(k + 1) * P], ident[:, :])
                return last

            def turn_weights():
                for t in range(NT):
                    last = tr(bank[1][:, t * P:(t + 1) * P], sw[:, t].rearrange("p e s -> p (e s)"), ident[:, :])
                return last

            def combine():
                for t in range(NT):
                    for half in range(2):
                        last = mm(bank[4 + 2 * t + half][:, :], swT[:, t, :], ysb[:, half * 512:(half + 1) * 512],
                                  start=False, stop=True, skip_group_check=True)
                return last

            def down(u=4):
                for k in range(4):
                    for half in range(2):
                        for e in range(2):
                            last = mm(bank[2 + half][e * CAP:(e + 1) * CAP, :], hT[:, k, e * CAP:(e + 1) * CAP],
                                      w3(u + e, 4)[:, k, half * 512:(half + 1) * 512],
                                      start=(k == 0), stop=(k == 3))
                return last

            base = [LANDED[MOE0 + j] for j in range(6)]
            ring_w = [w3(j, KC) for j in range(4)]
            side_w = [s.rearrange("p (k n) -> p k n", k=KC) for s in side]

            def pair(i, first_pair, last_pair):
                w = side_w if last_pair else ring_w
                if last_pair:
                    pe.wait_ge(S("side_gates"), 32)
                else:
                    for j in range(2):
                        pe.wait_ge(S(f"landed{j}"), 16 * i + base[j])
                pe.wait_ge(S("turned_copied"), 2 * i + 2)
                products(0, w[0:2]).then_inc(S("gates"), 1)
                if not first_pair:
                    pe.wait_ge(S("weights_copied"), i)
                    pe.wait_ge(S("y_copied"), 2 * i)
                    combine().then_inc(S("combined"), 1)
                if last_pair:
                    pe.wait_ge(S("side_ups"), 32)
                else:
                    for j in range(2, 4):
                        pe.wait_ge(S(f"landed{j}"), 16 * i + base[j])
                products(1, w[2:4]).then_inc(S("ups"), 1)
                if not last_pair:
                    pe.wait_ge(S("rows_in"), 16 * i + 32)
                    turn_pair().then_inc(S("rows_turned"), 1)
                pe.wait_ge(S("hidden"), i + 1)
                turn_hidden().then_inc(S("hid_turned"), 1)
                pe.wait_ge(S("weights_set"), i + 1)
                turn_weights().then_inc(S("weights_turned"), 1)
                if last_pair:
                    take(LAST0)
                    take(LAST0 + 1)
                else:
                    for j in range(4, 6):
                        pe.wait_ge(S(f"landed{j}"), 16 * i + base[j])
                pe.wait_ge(S("hT_ready"), i + 1)
                if not last_pair:
                    pe.wait_ge(S("turned_copied"), 2 * i + 4)
                down(LAST0 if last_pair else 4).then_inc(S("y_ready"), 1)

            pe.wait_ge(S("flag_set"), 1)
            for t in range(NT):
                for half in range(2):
                    mm(bank[4 + 2 * t + half][:, :], ident[:, :], h[:, t, half * 512:(half + 1) * 512],
                       start=True, stop=True)
            pe.wait_ge(S("rows_in"), 16)
            turn_pair().then_inc(S("rows_turned"), 1)
            pair(0, True, False)
            with pe.Fori(1, PAIRS - 1) as i:
                pair(i, False, False)
            pair(PAIRS - 1, False, True)
            pe.wait_ge(S("weights_copied"), PAIRS)
            pe.wait_ge(S("y_copied"), 2 * PAIRS)
            combine().then_inc(S("combined"), 1)

            pe.wait_ge(S("flag_set"), 1)
            over = pe.value_load(idx[0:1, 40:41], min_val=0, max_val=T)
            with pe.If(over > CAP):
                pe.sem_inc(S("over_y"), 1)
                with pe.Fori(0, (PASSES - 1) * PAIRS) as n:
                    pe.wait_ge(S("over_rows"), 16 * n + 16)
                    turn_pair().then_inc(S("over_turned"), 1)
                    pe.wait_ge(S("over_xgT"), n + 1)
                    pe.wait_ge(S("over_landed"), 96 * n + 96)
                    products(0, ring_w[0:2])
                    products(1, ring_w[2:4]).then_inc(S("over_gate_up"), 1)
                    pe.wait_ge(S("over_hidden"), n + 1)
                    turn_hidden().then_inc(S("over_hid"), 1)
                    pe.wait_ge(S("over_weights"), n + 1)
                    turn_weights().then_inc(S("over_weights_turned"), 1)
                    pe.wait_ge(S("over_hT"), n + 1)
                    down().then_inc(S("over_down"), 1)
                    pe.wait_ge(S("over_weights_copied"), n + 1)
                    pe.wait_ge(S("over_copied"), 2 * n + 2)
                    combine().then_inc(S("over_y"), 1)

            turn_rows(((0, P), (1, P)), "n3", xn2, 2)
            pe.wait_ge(S("norm_done"), 2 * ROWS["n3"] + 4)
            tiles = ((0, P), (P, P))

            def turn_qk(n):
                pe.wait_ge(S("roped"), n + 1)
                for t in range(NT):
                    m = 2 * n + t
                    if m >= 4:
                        pe.wait_ge(S("qk_copied"), m - 3)
                    for c in range(4):
                        last = tr(bank[4 + m % 4][:, c * P:(c + 1) * P], qk[n % 2][:, t, c * P:(c + 1) * P],
                                  ident[:, :])
                    last.then_inc(S("qk_turned"), 1)

            n_feat = [0]

            def gate_chunk():
                n = n_feat[0]
                u = B2_0 + 11 + n // 4
                if n % 4 == 0:
                    take(u)
                pe.wait_ge(S("evac"), n_out[0] - (1 if n >= 2 else 0))
                b = bank[n % 2]
                for k in range(KC):
                    last = mm(b[:, 0:T], w3(u, KC)[:, k, (n % 4) * P:(n % 4 + 1) * P], hn2[:, k, :],
                              start=(k == 0), stop=(k == KC - 1))
                last.then_inc(S("projected"), 1)
                n_feat[0] += 1
                n_out[0] += 1

            def scores(n):
                hd, tile = n // 2, 1 - n % 2
                keys = T if tile else P
                lo = (hd % 2) * HD
                if n >= 2:
                    pe.wait_ge(S("attn_cols"), n - 1)
                for g in range(NG):
                    c = g * 4 + hd // 2
                    col = g * keys
                    last = mm(bank[4 + 2 * (n % 2) + col // 512][:, col % 512:col % 512 + keys],
                              qkT[lo:lo + HD, c, tile * P:(tile + 1) * P], qkT[lo:lo + HD, 12 + c, 0:keys],
                              start=True, stop=True)
                last.then_inc(S("scores"), 1)

            for n in range(11):
                project_rows(B2_0 + n, tiles, hn2)
                if 1 <= n <= 6:
                    turn_qk(n - 1)
                if n == 9:
                    pe.wait_ge(S("ws_masked"), 1)
                    pe.wait_ge(S("qk_copied"), 12)
                    for g in range(SG):
                        last = tr(bank[6 + g // 4][:, (g % 4) * P:(g % 4 + 1) * P], wsr[:, g * P:(g + 1) * P],
                                  ident[:, :])
                    last.then_inc(S("ws_turned"), 1)
                    scores(0)

            for n in range(2 * AH):
                hd, tile = n // 2, 1 - n % 2
                nb = NG * (2 if tile else 1)
                gate_chunk()
                pe.wait_ge(S("probs_scaled"), n + 1)
                for b in range(nb):
                    last = tr(bank[2 + b // 4][:, (b % 4) * P:(b % 4 + 1) * P],
                              sc[n % 2][:, b * P:(b + 1) * P], ident[:, :])
                last.then_inc(S("probs_turned"), 1)
                if n == 0:
                    pe.wait_ge(S("ws_ready"), 2)
                if n + 1 < 2 * AH:
                    scores(n + 1)
                pe.wait_ge(S("PT_ready"), n + 1)
                for b in range(nb):
                    g, kt = (b // 2, b % 2) if tile else (b, 0)
                    last = mm(bank[4 + 2 * (n % 2)][(hd % 2) * HD:(hd % 2 + 1) * HD, 0:P],
                              vv[:, kt, g * 512 + hd * HD:g * 512 + (hd + 1) * HD], PTb[:, b * P:(b + 1) * P],
                              start=(b == 0), stop=(b == nb - 1))
                last.then_inc(S("pv"), 1)
            pe.wait_ge(S("attn_cols"), 2 * AH)
            pe.wait_ge(S("ln_rows"), 2)
            for t in range(NT):
                for g in range(SG):
                    last = mm(bank[4 + t][:, g * HD:(g + 1) * HD], wsT[:, g, :],
                              uv[:, t, 512 + g * HD:512 + (g + 1) * HD], start=True, stop=True)
                last.then_inc(S("mixed"), 1)
            pe.wait_ge(S("evac"), n_out[0])
            ua = B2_0 + 15
            for q, (src, lo) in enumerate(((aT, 0), (sT, 4))):
                if q == 1:
                    pe.wait_ge(S("sgu_rows"), 2)
                    for t in range(NT):
                        for c in range(4):
                            last = tr(bank[6 + t][:, c * P:(c + 1) * P], uv[:, t, c * P:(c + 1) * P], ident[:, :])
                        last.then_inc(S("sgu_turned"), 1)
                    pe.wait_ge(S("sT_ready"), 2)
                take(ua + q)
                for m in range(KC):
                    for k in range(4):
                        last = mm(bank[lo + m // 2][:, (m % 2) * T:(m % 2 + 1) * T],
                                  w3(ua + q, 4)[:, k, m * P:(m + 1) * P], src[:, k, :],
                                  start=(k == 0), stop=(k == 3))
                    if q == 1:
                        last.then_inc(S("proj_b"), 1)
                if q == 0:
                    last.then_inc(S("proj_a"), 1)
            out_projection(ua + 2, mT2, "merged2", 2, KC)

            turn_rows(((0, P), (1, P)), "n4", xn2, 2)
            pe.wait_ge(S("norm_done"), 2 * ROWS["n4"] + 4)
            uf = ua + 4
            for c in range(FC):
                u = uf + c // 2
                if c % 2 == 0:
                    take(u)
                if c >= 4:
                    pe.wait_ge(S("ff_cols"), c - 3)
                b = bank[4 + c % 4]
                for q in range(2):
                    for k in range(KC):
                        last = mm(b[:, q * T:(q + 1) * T],
                                  w3(u, 2 * KC)[:, KC * q + k, (c % 2) * P:(c % 2 + 1) * P], hn2[:, k, :],
                                  start=(k == 0), stop=(k == KC - 1))
                last.then_inc(S("ff"), 1)
            out_projection(uf + 11, ffT, "ff_cols", 6, FC)

        @block.scalar
        def _(act):
            A_ = nc.scalar.activation

            def rows(name):
                a = A[name]
                while len(a.shape) > 2:
                    a = a[0] if a.shape[0] == 1 else a.rearrange("a b c -> (a b) c")
                n = 1
                for d in a.shape:
                    n *= d
                if len(a.shape) == 2:
                    return a.rearrange("a (b c) -> (a b) c", c=P)
                return a.rearrange("(b c) -> b c", c=P)

            act.dma_start(meta[0:META, :], A["meta_tokens"]).then_inc(S("x_in0"), 16)
            for t in range(NT):
                act.dma_start(h[:, t, :], A["x"][0, t * P:(t + 1) * P, :]).then_inc(S(f"x_in{t + 1}"), 16)
            for name, n in VEC_ROWS:
                o = VEC_AT[name]
                act.dma_start(vecrows[o:o + n, :], rows(name)).then_inc(S("vec_loaded"), 16)
            act.dma_start(bias36[:, 0:4], A["b_group"].partition_broadcast(P).rearrange("p a b -> p (a b)")).then_inc(S("bias_loaded"), 16)
            act.dma_start(bias36[:, 4:36], A["b_router"].rearrange("a b c -> a (b c)").partition_broadcast(P)
                          .rearrange("p a b -> p (a b)")).then_inc(S("bias_loaded"), 16)
            act.dma_start(idx[:, 56:58], A["positions_2"][0].rearrange("(t p) -> p t", p=P), allow_slow_non_contiguous=True) \
                .then_inc(S("pos_loaded"), 16)
            act.sem_inc(S("params_issued"), 1)

            def squares(name, order, src, junk, col):
                for tile, n, ready in order:
                    act.wait_ge(S(ready[0]), ready[1])
                    A_(junk[0:n, tile, :], src[0:n, tile, :] if tile < NT else meta[0:n, :], ACT.Square,
                       accum_out=stat[0:n, col + tile:col + tile + 1]).then_inc(S("norm_sums"), 1)

            squares("n1", ((2, META, ("x_in0", 16)), (0, P, ("x_in1", 16)), (1, P, ("x_in2", 16))), h, xn, 0)

            n_out = [0]

            def evac(dst, func, parts=P, n=512, extra=None, b=None):
                k = n_out[0]
                n_out[0] += 1
                act.wait_ge(S("projected"), k + 1)
                src = bank[k % 4 if b is None else b][0:parts, 0:n]
                if extra is not None:
                    extra(src)
                A_(dst, src, func).then_inc(S("evac"), 1)

            act.wait_ge(S("lb_diff"), 1)
            A_(lbv, lbv, ACT.Exp).then_inc(S("lb_exp"), 1)
            act.wait_ge(S("lam_abs"), 1)
            A_(m2sp, m2sp, ACT.Exp).then_inc(S("lam_exp"), 1)
            act.wait_ge(S("lam_exp"), 1)
            A_(m2sp, m2sp, ACT.Ln, bias=1.0).then_inc(S("sp_log"), 1)
            for tile, n in ((2, META), (0, P), (1, P)):
                evac(v1[0:n, tile, :], ACT.Copy, n)
            act.dma_start(rw[:, :, 0:4], A["w_group"][0].rearrange("(k p) e -> p k e", p=P)).then_inc(S("rw_loaded"), 16)
            for g in range(GROUPS):
                act.dma_start(rw[:, :, 4 + EPG * g:4 + EPG * (g + 1)],
                              A["w_router"][0, g].rearrange("(k p) e -> p k e", p=P)).then_inc(S("rw_loaded"), 16)
            for c in range(4):
                evac(sf[:, c, :], ACT.Sigmoid, n=TT,
                     extra=lambda src: A_(kk[:, c, :], src, ACT.Sigmoid, scale=-1.0))
            act.wait_ge(S("f_ready"), 1)
            A_(sf, sf, ACT.Ln).then_inc(S("logf"), 1)
            for c in range(4):
                evac(qx[:, c, :], ACT.Copy, n=T)
            for part in range(2):
                act.wait_ge(S("end_diff"), part + 1)
                n = (META, P)[part]
                A_(W[part].rearrange("p (c t) -> p c t", c=4)[:, :, 0:n],
                   W[part].rearrange("p (c t) -> p c t", c=4)[:, :, 0:n], ACT.Exp).then_inc(S("end_decay"), 1)
            A_(egA, Gx[:, :, P - 1:P].rearrange("p c t -> p (c t)"), ACT.Exp).then_inc(S("eg"), 1)

            def level_exp(l):
                act.wait_ge(S("diff"), l + 1)
                A_(W[l % 2], W[l % 2], ACT.Exp).then_inc(S("decay"), 1)

            for c in range(4):
                evac(lx[:, c, 3:3 + TT], ACT.Copy, n=TT)
            level_exp(0)
            level_exp(1)
            for c in range(4):
                evac(lx[:, 4 + c, 3:3 + TT], ACT.Copy, n=TT)
            level_exp(2)
            level_exp(3)
            for c in range(4):
                evac(ly[:, c, :], ACT.Gelu_apprx_tanh, n=T)
            level_exp(4)
            level_exp(5)
            for c in range(4):
                evac(ly[:, 4 + c, :], ACT.Gelu_apprx_tanh, n=T)
            level_exp(6)
            for c in range(4):
                evac(og[:, c, :], ACT.Sigmoid, n=T)
            act.wait_ge(S("diff"), 8)
            A_(W[1], Gx.rearrange("p c t -> p (c t)"), ACT.Exp).then_inc(S("decay"), 1)
            for c in range(4):
                evac(ga[:, c, :], ACT.Sigmoid, n=T)
            act.wait_ge(S("o_ready"), 1)
            for c in range(2):
                A_(oT.rearrange("p c t -> p (c t)")[:, 512 * c:512 * c + 512], bank[4 + c][:, :], ACT.Copy)
                A_(W[0][:, 512 * c:512 * c + 512], bank[4 + c][:, :], ACT.Square).then_inc(S("o_squared"), 1)
            for c in range(4):
                evac(ga[:, 4 + c, :], ACT.Sigmoid, n=T)
            act.wait_ge(S("o_mean"), 1)
            A_(rsn, rsn, ACT.Sqrt).then_inc(S("o_root"), 1)
            for b in range(KC):
                for q in range(2):
                    n = 2 * b + q
                    act.wait_ge(S("lru_products"), n + 1)
                    A_((lrur, lrui)[q][:, b, :], bank[4 + n % 4][:, 0:TT], ACT.Sigmoid,
                       bias=V(("lru_b_r", "lru_b_i")[q], b)).then_inc(S("lru_gates"), 1)
            for c in range(4):
                evac(gb[:, c, :], ACT.Sigmoid, n=T)
            act.wait_ge(S("lru_gates"), 16)
            act.wait_ge(S("sp_ready"), 1)
            act.wait_ge(S("oa_ready"), 1)
            act.dma_start(g2b, A["norm2_g"].partition_broadcast(P).rearrange("p a b -> p (a b)")).then_inc(S("g2_loaded"), 16)
            for b in range(KC):
                A_(lrua[:, b, :], lrur[:, b, :], ACT.Exp, scale=m2sp[:, b:b + 1])
            for b in range(KC):
                last = A_(lrur[:, b, :], lrur[:, b, :], ACT.Tanh, scale=sp8[:, b:b + 1])
            last.then_inc(S("lru_decays"), 1)
            act.wait_ge(S("lru_under"), 1)
            A_(lrut, lrut, ACT.Sqrt).then_inc(S("lru_root"), 1)
            for c in range(4):
                evac(gb[:, 4 + c, :], ACT.Sigmoid, n=T)

            squares("n2", ((0, P, ("h_added", 1)), (1, P, ("h_added", 2))), h, hf, 24)
            for t in range(NT):
                act.wait_ge(S("norm_rows"), ROWS["n2"] + t + 1)
                act.dma_start(hf_d[t * P:(t + 1) * P, :], hf[:, t, :]).then_inc(S("hf_stored"), 16)
            act.wait_ge(S("route_diff"), 1)
            A_(rt[:, 64:72], rt[:, 64:72], ACT.Exp).then_inc(S("route_exp"), 1)
            act.wait_ge(S("route_diff2"), 1)
            A_(rt[:, 80:82], rt[:, 80:82], ACT.Exp).then_inc(S("route_exp"), 1)

            def silu():
                return A_(sg, bank[0][:, :], ACT.Silu)

            def copy_turned():
                return A_(xgT[:, 0:4, :], bank[2][:, 0:8 * CAP], ACT.Copy)

            def copy_hidden():
                return A_(hT, bank[0][:, :], ACT.Copy)

            act.wait_ge(S("rows_turned"), 1)
            copy_turned().then_inc(S("turned_copied"), 1)
            act.dma_start(fgb, A["final_g"].rearrange("(a b) -> a b", a=1).partition_broadcast(P)
                          .rearrange("p a b -> p (a b)")).then_inc(S("fg_loaded"), 16)

            def pair(i, last_pair):
                act.wait_ge(S("gates"), i + 1)
                not_zero(act, "hidden", i)
                silu().then_inc(S("silu"), 1)
                if not last_pair:
                    act.wait_ge(S("rows_turned"), i + 2)
                    copy_turned().then_inc(S("turned_copied"), 1)
                act.wait_ge(S("hid_turned"), i + 1)
                copy_hidden().then_inc(S("hT_ready"), 1)
                act.wait_ge(S("y_ready"), i + 1)
                A_(ysb[:, 0:512], bank[2][:, :], ACT.Copy).then_inc(S("y_copied"), 1)

            pair(0, False)
            with act.Fori(1, PAIRS - 1) as i:
                pair(i, False)
            pair(PAIRS - 1, True)
            act.wait_ge(S("flag_set"), 1)
            over = act.value_load(idx[0:1, 40:41], min_val=0, max_val=T)
            with act.If(over > CAP):
                with act.Fori(0, (PASSES - 1) * PAIRS) as n:
                    act.wait_ge(S("over_turned"), n + 1)
                    copy_turned().then_inc(S("over_half"), 1)
                    act.wait_ge(S("over_gate_up"), n + 1)
                    silu().then_inc(S("over_silu"), 1)
                    act.wait_ge(S("over_hid"), n + 1)
                    copy_hidden().then_inc(S("over_hT"), 1)
                    act.wait_ge(S("over_down"), n + 1)
                    A_(ysb[:, 0:512], bank[2][:, :], ACT.Copy).then_inc(S("over_copied"), 1)

            squares("f1", ((0, P, ("y_added", 1)), (1, P, ("y_added", 2))), h, hf, 48)
            squares("n3", ((0, P, ("x2_ready", 1)), (1, P, ("x2_ready", 2))), h, xn2, 50)
            act.wait_ge(S("angles"), 1)
            A_(rt[:, 0:32], rt[:, 0:32], ACT.Sin).then_inc(S("sincos"), 1)
            for n in range(6):
                for t in range(NT):
                    if n >= 2:
                        act.wait_ge(S("qk_turned"), 2 * (n - 1))
                    elif n == 0:
                        act.wait_ge(S("norm_done"), 2 * ROWS["n3"] + 4)
                    evac(qk[n % 2][:, t, :], ACT.Copy)
                if n >= 1:
                    for t in range(NT):
                        m = 2 * (n - 1) + t
                        act.wait_ge(S("qk_turned"), m + 1)
                        A_(qkT[:, 4 * (n - 1):4 * n, t * P:(t + 1) * P], bank[4 + m % 4][:, :]
                           .rearrange("p (c t) -> p c t", c=4), ACT.Copy).then_inc(S("qk_copied"), 1)
            for g in range(NG):
                for t in range(NT):
                    evac(vv[:, t, 512 * g:512 * g + 512], ACT.Copy)
                if g == 0:
                    for t in range(NT):
                        m = 10 + t
                        act.wait_ge(S("qk_turned"), m + 1)
                        A_(qkT[:, 20:24, t * P:(t + 1) * P], bank[4 + m % 4][:, :]
                           .rearrange("p (c t) -> p c t", c=4), ACT.Copy).then_inc(S("qk_copied"), 1)
            act.wait_ge(S("x2_ready"), NT)
            act.dma_start(wsr.rearrange("p (g t) -> p g t", g=SG), A["w_spatial_2"][0].rearrange("g t s -> t g s")) \
                .then_inc(S("ws_loaded"), 16)
            act.wait_ge(S("qk_turned"), 12)
            act.dma_start(lngb[:, 0:512], A["sgu_ln_g_2"].partition_broadcast(P).rearrange("p a b -> p (a b)")).then_inc(S("ln_loaded"), 16)
            act.dma_start(lngb[:, 512:1024], A["sgu_ln_b_2"].partition_broadcast(P).rearrange("p a b -> p (a b)")).then_inc(S("ln_loaded"), 16)
            for u in range(2):
                for t in range(NT):
                    evac(uv[:, t, 512 * u:512 * u + 512], ACT.Gelu)

            def gate_evac():
                c = n_out[0] - GATE0
                evac(gate[:, c, :], ACT.Copy, n=T, b=c % 2)

            GATE0 = n_out[0]

            def exp_scores(n):
                keys = NG * (T if n % 2 == 0 else P)
                c = 100 + 4 * (n % 2)
                act.wait_ge(S("scored"), n + 1)
                A_(sc[n % 2][:, 0:keys], sc[n % 2][:, 0:keys], ACT.Exp, scale=HD ** -0.5, bias=stat[:, c:c + 1],
                   accum_out=stat[:, c + 1:c + 2]).then_inc(S("probs"), 1)

            exp_scores(0)
            for n in range(2 * AH):
                tile = 1 - n % 2
                gate_evac()
                act.wait_ge(S("probs_turned"), n + 1)
                if n >= 1:
                    act.wait_ge(S("pv"), n)
                w = 512 if tile else NG * P
                A_(PTb[:, 0:w], bank[2][:, 0:w], ACT.Copy).then_inc(S("PT_half" if tile else "PT_ready"), 1)
                if n + 1 < 2 * AH:
                    exp_scores(n + 1)
                act.wait_ge(S("pv"), n + 1)
                hd = n // 2
                half = slice((hd % 2) * HD, (hd % 2 + 1) * HD)
                A_(aT[half, hd // 2, tile * P:(tile + 1) * P], bank[4 + 2 * (n % 2)][half, 0:P], ACT.Copy) \
                    .then_inc(S("attn_cols"), 1)
            act.wait_ge(S("evac"), n_out[0])
            for q in range(2):
                A_(gate[:, KC * q:KC * q + KC, :], gate[:, KC * q:KC * q + KC, :], ACT.Sigmoid) \
                    .then_inc(S("gates_sigmoid"), 1)
            squares("n4", ((0, P, ("x3_added", 1)), (1, P, ("x3_added", 2))), h, xn2, 64)
            for c in range(FC):
                act.wait_ge(S("ff"), c + 1)
                if c >= 4:
                    act.wait_ge(S("ff_cols"), c - 3)
                A_(sgf[:, c % 4, :], bank[4 + c % 4][:, 0:T], ACT.Silu).then_inc(S("ff_silu"), 1)
                if c == 4:
                    act.dma_start(fgb2, A["final_g_2"].rearrange("(a b) -> a b", a=1).partition_broadcast(P)
                                  .rearrange("p a b -> p (a b)")).then_inc(S("fg2_loaded"), 16)
            squares("f2", ((0, P, ("x4_added", 1)), (1, P, ("x4_added", 2))), h, outr, 88)

        @block.vector
        def _(dve):
            v = nc.vector
            n_link = [0]

            def link(ins):
                n_link[0] += 1
                ins.then_inc(S("dve_chain"), 1)
                dve.wait_ge(S("dve_chain"), n_link[0])

            def norm_rows(name, order, src, dst, col, g=None, only=None):
                for j, (tile, n) in enumerate(order):
                    if only not in (None, j):
                        continue
                    dve.wait_ge(S("norm_rstd"), STATS[name] + j + 1)
                    r = stat[0:n, col + 16 + tile:col + 17 + tile]
                    if g is None:
                        rows = src[0:n, tile, :] if tile < NT else meta[0:n, :]
                        v.tensor_scalar(dst[0:n, tile, :], rows, r, None, ALU.mult) \
                            .then_inc(S("norm_rows"), 1)
                    else:
                        v.scalar_tensor_tensor(out=dst[0:n, tile, :], in0=src[0:n, tile, :], scalar=r, in1=g,
                                               op0=ALU.mult, op1=ALU.mult).then_inc(S("norm_rows"), 1)

            def turned_out(name, order, dst, g, only=None):
                for j, (lo, n) in enumerate(order):
                    if only not in (None, j):
                        continue
                    for half in range(2):
                        dve.wait_ge(S("norm_turned"), 2 * ROWS[name] + 2 * j + half + 1)
                        src = bank[2 * j + half][:, 0:4 * n].rearrange("p (c t) -> p c t", c=4)
                        o = dst[:, 4 * half:4 * half + 4, lo:lo + n]
                        if g is None:
                            v.tensor_copy(o, src).then_inc(S("norm_done"), 1)
                        else:
                            v.tensor_tensor(o, src, bc(V(g, 4 * half, 4), [P, 4, n], 2), ALU.mult) \
                                .then_inc(S("norm_done"), 1)

            dve.wait_ge(S("vec_turned"), 1)
            link(v.tensor_copy(vec[:, :], bank[7][:, 0:NVR]))
            norm_rows("n1", ((2, META), (0, P), (1, P)), h, xn, 0)
            turned_out("n1", ((0, META), (META, P), (META + P, P)), hnT, "norm1_g")

            v.tensor_tensor(lbv, V("hg_lower_bounds", 4, 4), V("hg_lower_bounds", 0, 4), ALU.subtract) \
                .then_inc(S("lb_diff"), 1)
            dve.wait_ge(S("lb_exp"), 1)
            link(v.tensor_scalar(omlb, lbv, 1.0, None, ALU.add))
            link(v.reciprocal(lbv, omlb))
            link(v.tensor_scalar(omlb, lbv, -1.0, 1.0, ALU.mult, ALU.add))
            lam = V("lru_lambda", 0, 8)
            link(v.tensor_scalar(tmp8, lam, -1.0, None, ALU.mult))
            v.tensor_tensor(m2sp, tmp8, lam, ALU.min).then_inc(S("lam_abs"), 1)
            link(v.tensor_scalar(tmp8, tmp8, 0.0, None, ALU.max))
            dve.wait_ge(S("sp_log"), 1)
            link(v.tensor_tensor(tmp8, tmp8, m2sp, ALU.add))
            v.tensor_scalar(sp8, tmp8, 8.0, None, ALU.mult)
            v.tensor_scalar(m2sp, tmp8, -8.0, None, ALU.mult).then_inc(S("sp_ready"), 1)

            dve.wait_ge(S("iotas"), 2)
            link(v.tensor_tensor(maskw[:, 6, :], idx[:, 60:61].to_broadcast([P, P]), maskw[:, 7, :], ALU.bitwise_xor))
            link(v.tensor_tensor(maskw[:, 5, :], maskw[:, 7, :], idx[:, 60:61].to_broadcast([P, P]), ALU.is_gt))
            link(v.tensor_copy(maskw[:, 7, :], maskw[:, 6, :]))
            link(v.tensor_copy(PT[:, 7, :].bitcast(I32), maskw[:, 5, :]))
            tgt = PT[:, 7, :].bitcast(I32)
            for l, m in enumerate(LEVELS):
                link(v.tensor_scalar(maskw[:, l, :], maskw[:, 7, :], m, None, ALU.is_ge))
                link(v.tensor_tensor(maskw[:, l, :], maskw[:, l, :], tgt, ALU.mult))
                link(v.tensor_scalar(PT[:, 6, :].bitcast(I32), maskw[:, 7, :], 2 * m, None, ALU.is_lt))
                link(v.tensor_tensor(maskw[:, l, :], maskw[:, l, :], PT[:, 6, :].bitcast(I32), ALU.mult))
            link(v.tensor_scalar(maskw[:, 7, :], maskw[:, 7, :], 0, None, ALU.is_equal))
            dve.wait_ge(S("pool_chain"), 5)
            link(v.memset(PT, 0.0))

            dve.wait_ge(S("evac"), 7)
            for c in range(HEADS):
                last = v.tensor_scalar(sf[:, c, :], sf[:, c, :], omlb[:, c:c + 1], lbv[:, c:c + 1],
                                       ALU.mult, ALU.add)
            last.then_inc(S("f_ready"), 1)
            for c in range(HEADS):
                last = v.tensor_scalar(kk[:, c, :], kk[:, c, :], omlb[:, c:c + 1], None, ALU.mult)
            link(last)
            link(v.tensor_copy(kx, kk[:, :, META:TT]))
            dve.wait_ge(S("logf"), 1)
            for c in range(HEADS):
                v.tensor_tensor_scan(Gm[:, c, :], ones[:, 0:META], sf[:, c, 0:META], 0.0, ALU.mult, ALU.add)
                for t in range(NT):
                    last = v.tensor_tensor_scan(Gx[:, c, t * P:(t + 1) * P], ones[:, :],
                                                sf[:, c, META + t * P:META + (t + 1) * P], 0.0, ALU.mult, ALU.add)
            link(last)
            for part in range(2):
                n = (META, P)[part]
                G = (Gm, Gx)[part]
                k = (kk, kx)[part]
                d = W[part].rearrange("p (c t) -> p c t", c=4)[:, :, 0:n]
                v.tensor_tensor(d, G[:, :, n - 1:n].to_broadcast([P, 4, n]), G[:, :, 0:n], ALU.subtract) \
                    .then_inc(S("end_diff"), 1)
            for part in range(2):
                n = (META, P)[part]
                k = (kk, kx)[part]
                d = W[part].rearrange("p (c t) -> p c t", c=4)[:, :, 0:n]
                dve.wait_ge(S("end_decay"), part + 1)
                v.tensor_tensor(kE[:, 0:512].rearrange("p (c t) -> p c t", c=4)[:, :, 0:n], k[:, :, 0:n], d, ALU.mult) \
                    .then_inc(S("k_end"), 1)
                dve.wait_ge(S("k_turned"), part + 1)
                v.tensor_copy(kT[0:n, part, :], bank[4][0:n, :]).then_inc(S("kT_ready"), 1)
                dve.wait_ge(S("kv"), part + 1)
                if part == 0:
                    v.tensor_copy(St[:, 0, :, :], bank[5][:, :].rearrange("p (h v) -> p h v", h=4)) \
                        .then_inc(S("state"), 1)
                else:
                    dve.wait_ge(S("eg"), 1)
                    dve.wait_ge(S("state"), 1)
                    for hd in range(HEADS):
                        last = v.scalar_tensor_tensor(out=St[:, 1, hd, :], in0=St[:, 0, hd, :],
                                                      scalar=egA[:, hd:hd + 1], in1=bank[5][:, hd * P:(hd + 1) * P],
                                                      op0=ALU.mult, op1=ALU.add)
                    last.then_inc(S("state"), 1)

            def seg(ap, m):
                return ap.rearrange("p (n w) -> p n w", w=2 * m)

            Gf = Gx.rearrange("p c t -> p (c t)")
            qf = qx.rearrange("p c t -> p (c t)")
            kf = kx.rearrange("p c t -> p (c t)")

            def diff(l):
                m = LEVELS[l]
                n = 512 // m
                mid = seg(Gf, m)[:, :, m - 1:m].to_broadcast([P, n, m])
                w = seg(W[l % 2], m)
                v.tensor_tensor(w[:, :, m:2 * m], seg(Gf, m)[:, :, m:2 * m], mid, ALU.subtract)
                v.tensor_tensor(w[:, :, 0:m], mid, seg(Gf, m)[:, :, 0:m], ALU.subtract).then_inc(S("diff"), 1)

            def scaled(l):
                m = LEVELS[l]
                dve.wait_ge(S("decay"), l + 1)
                if l >= 2:
                    dve.wait_ge(S("levels"), l - 1)
                w = seg(W[l % 2], m)
                o = seg(z[l % 2], m)
                v.tensor_tensor(o[:, :, m:2 * m], seg(qf, m)[:, :, m:2 * m], w[:, :, m:2 * m], ALU.mult)
                v.tensor_tensor(o[:, :, 0:m], seg(kf, m)[:, :, 0:m], w[:, :, 0:m], ALU.mult).then_inc(S("z_ready"), 1)

            def pick(l):
                dve.wait_ge(S("levels"), l + 1)
                if l:
                    dve.wait_ge(S("picked"), l)
                for b in range(2):
                    last = v.copy_predicated(PT[:, 4 * b:4 * b + 4, :],
                                             bc(maskw[:, l, :], [P, 4, P], 1),
                                             bank[4 + 2 * (l % 2) + b][:, :].rearrange("p (c t) -> p c t", c=4))
                last.then_inc(S("picked"), 1)

            dve.wait_ge(S("evac"), 11)
            dve.wait_ge(S("k_end"), 2)
            dve.wait_ge(S("k_turned"), 2)
            diff(0)
            for l in range(7):
                if l < 6:
                    if l >= 1:
                        dve.wait_ge(S("z_ready"), l)
                    diff(l + 1)
                scaled(l)
                if l >= 1:
                    pick(l - 1)
            v.memset(pdt[:, 1:2], 0.0).then_inc(S("diff"), 1)
            pick(6)
            pick(7)
            dve.wait_ge(S("decay"), 8)
            v.tensor_tensor(qf, qf, W[1], ALU.mult).then_inc(S("qe_ready"), 1)

            for c in range(KC):
                dve.wait_ge(S("evac"), 12 + c)
                link(v.tensor_scalar(xc[:, c, :], lx[:, c, 0:TT], V("conv_w", c), V("conv_b", c), ALU.mult, ALU.add))
                for j in range(1, 4):
                    ins = v.scalar_tensor_tensor(out=xc[:, c, :], in0=lx[:, c, j:j + TT],
                                                 scalar=V("conv_w", 8 * j + c), in1=xc[:, c, :],
                                                 op0=ALU.mult, op1=ALU.add)
                    if j < 3:
                        link(ins)
                    else:
                        ins.then_inc(S("conv"), 1)
            of = oT.rearrange("p c t -> p (c t)")
            dve.wait_ge(S("o_sums"), 1)
            for c in range(2):
                last = v.tensor_scalar(rsn[:, 512 * c:512 * c + 512], bank[6 + c][:, :], 1.0 / P, EPS, ALU.mult, ALU.add)
            last.then_inc(S("o_mean"), 1)
            dve.wait_ge(S("o_mean"), 1)
            dve.wait_ge(S("o_root"), 1)
            link(v.reciprocal(rsn, rsn))
            dve.wait_ge(S("o_squared"), 2)
            link(v.tensor_tensor(of, of, rsn, ALU.mult))
            for c in range(HEADS):
                last = v.scalar_tensor_tensor(out=oT[:, c, :], in0=oT[:, c, :], scalar=V("hg_norm_g", c),
                                              in1=og[:, c, :], op0=ALU.mult, op1=ALU.mult)
            last.then_inc(S("oa_ready"), 1)
            dve.wait_ge(S("lru_decays"), 1)
            link(v.tensor_tensor(lrut, lrua, lrua, ALU.mult))
            for c in range(2):
                last = v.scalar_tensor_tensor(out=lrut[:, 4 * c:4 * c + 4, :], in0=lrut[:, 4 * c:4 * c + 4, :],
                                              scalar=1.0, in1=lrur[:, 4 * c:4 * c + 4, :], op0=ALU.add, op1=ALU.mult)
            last.then_inc(S("lru_under"), 1)
            link(v.tensor_tensor(lrui, lrui, xc, ALU.mult))
            dve.wait_ge(S("lru_root"), 1)
            link(v.tensor_tensor(lrui, lrui, lrut, ALU.mult))
            for c in range(KC):
                last = v.tensor_tensor_scan(lrut[:, c, :], lrua[:, c, :], lrui[:, c, :], 0.0, ALU.mult, ALU.add)
            link(last)
            dve.wait_ge(S("evac"), 27)
            v.tensor_tensor(ly, ly, lrut[:, :, META:TT], ALU.mult).then_inc(S("ob_ready"), 1)

            def merge(name_a, name_b, done, ga_, gb_, dst, tmp):
                dve.wait_ge(S(name_a), 1)
                for m in range(KC):
                    dve.wait_ge(S(name_b), 2 * (m // 2) + 2)
                    cols = slice((m % 2) * T, (m % 2 + 1) * T)
                    v.tensor_tensor(tmp[:, 0:T], ga_[:, m, :], bank[m // 2][:, cols], ALU.mult)
                    link(v.tensor_tensor(tmp[:, T:2 * T], gb_[:, m, :], bank[4 + m // 2][:, cols], ALU.mult))
                    v.tensor_tensor(dst[:, m, :], tmp[:, 0:T], tmp[:, T:2 * T], ALU.add).then_inc(S(done), 1)
                    dve.wait_ge(S(done), m + 1)

            dve.wait_ge(S("evac"), 47)
            merge("up_a", "up_b", "merged", ga, gb, mT, W[0])

            def add_rows(t, ready, done):
                dve.wait_ge(S(ready), t + 1)
                for half in range(2):
                    hh = h[:, t, half * 512:(half + 1) * 512]
                    ins = v.tensor_tensor(hh, hh, bank[2 * t + half][:, :], ALU.add)
                ins.then_inc(S(done), 1)

            def add_and_norm(ready, done, name, rows, col, g_rows, dst, g_cols):
                order, turned = ((0, P), (1, P)), ((0, P), (P, P))
                add_rows(0, ready, done)
                norm_rows(name, order, h, rows, col, g=g_rows, only=0)
                add_rows(1, ready, done)
                turned_out(name, turned, dst, g_cols, only=0)
                norm_rows(name, order, h, rows, col, g=g_rows, only=1)
                turned_out(name, turned, dst, g_cols, only=1)

            dve.wait_ge(S("g2_loaded"), 16)
            add_and_norm("out_merged", "h_added", "n2", hf, 24, g2b, hfT, None)

            dve.wait_ge(S("logits"), 2)
            dve.wait_ge(S("bias_loaded"), 32)
            dve.wait_ge(S("route_consts"), 5)
            for t in range(NT):
                last = v.tensor_tensor(lg[:, t, :], bank[4 + t][:, 0:36], bias36, ALU.add)
            link(last)
            o = [100]

            def r2(n):
                a = rt[:, o[0]:o[0] + 2 * n].rearrange("p (t e) -> p t e", t=2)
                o[0] += 2 * n
                return a

            def one_hot(dst, vals, n, scratch, vmax, vidx):
                io = bc(iota32[:, 0:n], [P, 2, n], 1)
                link(v.tensor_reduce(vmax, vals, AX_X, ALU.max))
                link(v.tensor_tensor(scratch, vals, vmax.to_broadcast([P, 2, n]), ALU.is_lt))
                link(v.scalar_tensor_tensor(out=scratch, in0=scratch, scalar=1000.0, in1=io, op0=ALU.mult, op1=ALU.add))
                link(v.tensor_reduce(vidx, scratch, AX_X, ALU.min))
                link(v.tensor_tensor(dst, vidx.to_broadcast([P, 2, n]), io, ALU.is_equal))

            gm, gi, m1, i1, m2, i2 = (r2(1) for _ in range(6))
            goh, gs = r2(4), r2(4)
            one_hot(goh, lg[:, :, 0:4], 4, gs, gm, gi)
            ge = rt[:, 64:72].rearrange("p (t e) -> p t e", t=2)
            v.tensor_tensor(ge, lg[:, :, 0:4], gm.to_broadcast([P, 2, 4]), ALU.subtract).then_inc(S("route_diff"), 1)
            big, es = r2(32), r2(32)
            E0 = o[0]
            e1, e2 = r2(32), r2(32)
            big4 = big.rearrange("p t (g e) -> p t g e", g=GROUPS)
            for t in range(NT):
                last = v.tensor_scalar(big4[:, t], bc(goh[:, t, :], [P, GROUPS, EPG], 2), -1.0, -NEG, ALU.add, ALU.mult)
            link(last)
            for t in range(NT):
                last = v.tensor_tensor(es[:, t].rearrange("p (g e) -> p g e", g=GROUPS),
                                       lg[:, t, 4:36].rearrange("p (g e) -> p g e", g=GROUPS),
                                       bc(goh[:, t, :], [P, GROUPS, EPG], 2), ALU.mult)
            link(last)
            link(v.tensor_tensor(big, big, es, ALU.add))
            one_hot(e1, big, 32, es, m1, i1)
            link(v.scalar_tensor_tensor(out=big, in0=e1, scalar=2.0 * NEG, in1=big, op0=ALU.mult, op1=ALU.add))
            one_hot(e2, big, 32, es, m2, i2)
            M = rt[:, 0:64].rearrange("p (t e) -> p t e", t=2)
            v.tensor_tensor(M, e1, e2, ALU.add).then_inc(S("chosen"), 1)
            dd = rt[:, 80:82].rearrange("p (t e) -> p t e", t=2)
            v.tensor_tensor(dd, m2, m1, ALU.subtract).then_inc(S("route_diff2"), 1)
            chosen = rt[:, E0:E0 + 128].rearrange("p (k e) -> p k e", k=4)
            per = rt[:, o[0]:o[0] + 128].rearrange("p (k e) -> p k e", k=4)
            o[0] += 128
            half0, pair0, rank, passes, place, column = (
                rt[:, o[0] + 4 * q:o[0] + 4 * q + 4].unsqueeze(2) for q in range(6))
            o[0] += 24
            cnt = rt[:, o[0]:o[0] + 1]
            s2, p1 = (rt[:, o[0] + 2 + 2 * q:o[0] + 4 + 2 * q].unsqueeze(2) for q in range(2))
            assert o[0] + 6 <= 644
            for dst, table in ((half0, half_of), (pair0, pair_of)):
                link(v.tensor_tensor(per, chosen, bc(table, [P, 4, 32], 1), ALU.mult))
                link(v.tensor_reduce(dst, per, AX_X, ALU.add))
            dve.wait_ge(S("places"), 1)
            for j in range(2):
                last = v.tensor_tensor(per[:, 2 * j:2 * j + 2, :], chosen[:, 2 * j:2 * j + 2, :],
                                       bank[6][:, 0:64].rearrange("p (t e) -> p t e", t=2), ALU.mult)
            link(last)
            link(v.tensor_reduce(rank, per, AX_X, ALU.add))
            link(v.tensor_scalar(passes, rank, float(CAP), None, ALU.is_ge))
            for a in range(2, PASSES):
                link(v.scalar_tensor_tensor(out=passes, in0=rank, scalar=float(CAP * a), in1=passes,
                                            op0=ALU.is_ge, op1=ALU.add))
            v.tensor_tensor(half0, half0, rank, ALU.add)
            link(v.scalar_tensor_tensor(out=column, in0=passes, scalar=float(PAIRS), in1=pair0,
                                        op0=ALU.mult, op1=ALU.add))
            for q in range(4):
                last = v.tensor_scalar(list_hot[:, q, :], iota128[:, 0:PASSES * PAIRS], column[:, q, :],
                                       tokid[:, q % 2:q % 2 + 1], ALU.is_equal, ALU.mult)
            last.then_inc(S("list_hot"), 1)
            link(v.scalar_tensor_tensor(out=place, in0=passes, scalar=-float(CAP), in1=half0,
                                        op0=ALU.mult, op1=ALU.add))
            v.tensor_tensor(slot_hot, bc(iota128, [P, 4, P], 1), place.to_broadcast([P, 4, P]), ALU.is_equal) \
                .then_inc(S("slot_hot"), 1)
            dve.wait_ge(S("lists"), 1)
            v.tensor_copy(lists, bank[7][:, 0:PASSES * PAIRS]).then_inc(S("lists_set"), 1)
            expert_place = big
            link(v.scalar_tensor_tensor(out=big, in0=bank[6][:, 0:64].rearrange("p (t e) -> p t e", t=2),
                                        scalar=1.0, in1=M, op0=ALU.add, op1=ALU.mult))
            link(v.tensor_scalar(big, big, -1.0, None, ALU.add))
            link(v.tensor_reduce(cnt, bank[6][:, 64:96], AX_X, ALU.max))
            v.tensor_copy(idx[:, 40:41], cnt).then_inc(S("flag_set"), 1)
            dve.wait_ge(S("route_exp"), 2)
            wt = rt[:, 84:88].rearrange("p (t k) -> p t k", t=2)
            link(v.tensor_reduce(p1, ge, AX_X, ALU.add))
            link(v.tensor_scalar(s2, dd, 1.0, None, ALU.add))
            link(v.tensor_tensor(s2, s2, p1, ALU.mult))
            link(v.reciprocal(wt[:, :, 0:1], s2))
            link(v.tensor_tensor(wt[:, :, 1:2], wt[:, :, 0:1], dd, ALU.mult))
            expert_weight = es
            link(v.tensor_tensor(es, e1, wt[:, :, 0:1].to_broadcast([P, 2, 32]), ALU.mult))
            link(v.tensor_tensor(e2, e2, wt[:, :, 1:2].to_broadcast([P, 2, 32]), ALU.mult))
            link(v.tensor_tensor(es, es, e2, ALU.add))

            def set_weights(e, hot, hot_count, done):
                def wide(a):
                    return a[:, :, bass.ds(e, 2)].unsqueeze(3).to_broadcast([P, NT, 2, CAP])

                slots = iota128[:, 0:CAP].unsqueeze(1).unsqueeze(1).to_broadcast([P, NT, 2, CAP])
                v.tensor_tensor(sw, slots, wide(expert_place), ALU.is_equal).then_inc(S(hot), 1)
                dve.wait_ge(S(hot), hot_count)
                v.tensor_tensor(sw, sw, wide(expert_weight), ALU.mult).then_inc(S(done), 1)

            def copy_weights():
                return v.tensor_copy(swT, bank[1][:, 0:NT * P].rearrange("p (t n) -> p t n", t=NT))

            def copy_turned():
                return v.tensor_copy(xgT[:, 4:8, :], bank[3][:, 0:8 * CAP].rearrange("p (c t) -> p c t", c=4))

            def hidden():
                return v.tensor_tensor(hid, sg, bank[1][:, :], ALU.mult)

            set_weights(0, "slot_found", 1, "weights_set")
            dve.wait_ge(S("rows_turned"), 1)
            copy_turned().then_inc(S("turned_copied"), 1)

            def pair(i, last_pair):
                dve.wait_ge(S("silu"), i + 1)
                dve.wait_ge(S("ups"), i + 1)
                hidden().then_inc(S("hidden"), 1)
                if not last_pair:
                    dve.wait_ge(S("rows_turned"), i + 2)
                    copy_turned().then_inc(S("turned_copied"), 1)
                dve.wait_ge(S("weights_turned"), i + 1)
                copy_weights().then_inc(S("weights_copied"), 1)
                if not last_pair:
                    set_weights(2 * i + 2, "slot_found", i + 2, "weights_set")
                dve.wait_ge(S("y_ready"), i + 1)
                v.tensor_copy(ysb[:, 512:1024], bank[3][:, :]).then_inc(S("y_copied"), 1)

            pair(0, False)
            dve.wait_ge(S("pos_loaded"), 16)
            link(v.tensor_copy(pdt[:, 6:8], idx[:, 56:58]))
            ang = rt[:, 0:32].rearrange("p (q t f) -> p q t f", q=2, t=2)
            trn = rt[:, 32:64].rearrange("p (q t f) -> p q t f", q=2, t=2)
            for q in range(2):
                for f in range(8):
                    last = v.tensor_scalar(ang[:, q, :, f], pdt[:, 6:8], INV_FREQ[f], None, ALU.mult)
            link(last)
            MAGIC = 12582912.0
            C1, C2, C3 = 6.28125, 0.0019350051879882812, 3.0197e-07
            two_pi = 2 * np.pi
            C3 = float(np.float32(two_pi - C1 - C2))
            for q in range(2):
                link(v.tensor_scalar(trn[:, q], ang[:, q], float(1 / two_pi), 0.25 * (1 - q), ALU.mult, ALU.add))
            link(v.tensor_scalar(trn, trn, MAGIC, None, ALU.add))
            link(v.tensor_scalar(trn, trn, -MAGIC, None, ALU.add))
            for C in (C1, C2, C3):
                for q in range(2):
                    last = v.scalar_tensor_tensor(out=ang[:, q], in0=trn[:, q], scalar=-C, in1=ang[:, q],
                                                  op0=ALU.mult, op1=ALU.add)
                link(last)
            link(v.tensor_scalar(ang[:, 0], ang[:, 0], float(np.pi / 2), None, ALU.add))
            v.tensor_scalar(rt[:, 0:32], rt[:, 0:32], 3.1415925, -3.1415925, ALU.min, ALU.max).then_inc(S("angles"), 1)
            with dve.Fori(1, PAIRS - 1) as i:
                pair(i, False)
            pair(PAIRS - 1, True)
            dve.wait_ge(S("flag_set"), 1)
            over = dve.value_load(idx[0:1, 40:41], min_val=0, max_val=T)
            with dve.If(over > CAP):
                for a in range(PASSES - 1):
                    if a:
                        dve.wait_ge(S("over_weights"), a * PAIRS)
                    v.tensor_scalar(big, big, -float(CAP), None, ALU.add).then_inc(S("over_places"), 1)
                    dve.wait_ge(S("over_places"), a + 1)
                    with dve.Fori(0, PAIRS) as i:
                        n = i + a * PAIRS
                        set_weights(2 * i, "over_found", n + 1, "over_weights")
                        dve.wait_ge(S("over_half"), n + 1)
                        copy_turned().then_inc(S("over_xgT"), 1)
                        dve.wait_ge(S("over_silu"), n + 1)
                        hidden().then_inc(S("over_hidden"), 1)
                        dve.wait_ge(S("over_weights_turned"), n + 1)
                        copy_weights().then_inc(S("over_weights_copied"), 1)
                        dve.wait_ge(S("over_down"), n + 1)
                        v.tensor_copy(ysb[:, 512:1024], bank[3][:, :]).then_inc(S("over_copied"), 1)
                dve.wait_ge(S("over_y"), (PASSES - 1) * PAIRS + 1)

            dve.wait_ge(S("combined"), PAIRS)
            for t in range(NT):
                for half in range(2):
                    last = v.tensor_copy(h[:, t, half * 512:(half + 1) * 512], bank[4 + 2 * t + half][:, :])
                last.then_inc(S("y_added"), 1)
            dve.wait_ge(S("fg_loaded"), 16)
            for t in range(NT):
                dve.wait_ge(S("norm_rstd"), STATS["f1"] + t + 1)
                v.scalar_tensor_tensor(out=h[:, t, :], in0=h[:, t, :], scalar=stat[:, 64 + t:65 + t], in1=fgb,
                                       op0=ALU.mult, op1=ALU.mult).then_inc(S("x2_ready"), 1)
            norm_rows("n3", ((0, P), (1, P)), h, xn2, 50)
            turned_out("n3", ((0, P), (P, P)), hn2, "norm1_g_2")

            dve.wait_ge(S("diff_iota"), 1)
            di = scw[:, 0:T].bitcast(I32)
            lowi = scw[:, T:2 * T].bitcast(I32)
            lowf = scw[:, 2 * T:3 * T]
            for g, dil in ((1, 4), (2, 16)):
                link(v.tensor_scalar(lowi, di, dil - 1, None, ALU.bitwise_and))
                link(v.tensor_scalar(lowf, lowi, 0.0, NEG, ALU.is_gt, ALU.mult))
                for o_, n in ((T * g, T), (NG * T + P * g, P)):
                    link(v.tensor_tensor(amask[:, o_:o_ + n], amask[:, o_:o_ + n], lowf[:, 0:n], ALU.add))

            dve.wait_ge(S("sincos"), 1)
            cos = ang[:, 0]
            sin = ang[:, 1]
            for n in range(6):
                dve.wait_ge(S("evac"), 47 + 2 * n + 2)
                for t in range(NT):
                    x = qk[n % 2][:, t, :].rearrange("p (h d) -> p h d", h=AH)
                    x1, x2 = x[:, :, 0:8], x[:, :, 8:16]
                    c8 = bc(cos[:, t, :], [P, AH, 8], 1)
                    s8 = bc(sin[:, t, :], [P, AH, 8], 1)
                    a, b, c, d = (rtmp[:, k, 64 * t:64 * t + 64].rearrange("p (h d) -> p h d", h=AH) for k in range(4))
                    v.tensor_tensor(a, x1, c8, ALU.mult)
                    v.tensor_tensor(b, x2, s8, ALU.mult)
                    v.tensor_tensor(c, x2, c8, ALU.mult)
                    link(v.tensor_tensor(d, x1, s8, ALU.mult))
                    v.tensor_tensor(x1, a, b, ALU.subtract)
                    last = v.tensor_tensor(x2, c, d, ALU.add)
                last.then_inc(S("roped"), 1)

            dve.wait_ge(S("ws_turned"), 1)
            for g2 in range(2):
                v.tensor_copy(wsT[:, 4 * g2:4 * g2 + 4, :], bank[6 + g2][:, :].rearrange("p (g t) -> p g t", g=4)) \
                    .then_inc(S("ws_ready"), 1)
            bn = rt[:, 64:80].rearrange("p (t n) -> p t n", t=2)

            def gate_stats():
                dve.wait_ge(S("evac"), 47 + 22)
                for t in range(NT):
                    link(v.bn_stats(bn[:, t, 0:6], uv[:, t, 512:1024]))
                    link(v.bn_aggr(bn[:, t, 6:8], bn[:, t, 0:6]))
                    v.tensor_copy(stat[:, 56 + t:57 + t], bn[:, t, 7:8]).then_inc(S("norm_sums"), 1)

            def gate_rows(t):
                dve.wait_ge(S("ln_loaded"), 32)
                dve.wait_ge(S("norm_rstd"), STATS["ln"] + t + 1)
                x = uv[:, t, 512:1024]
                link(v.tensor_scalar(x, x, bn[:, t, 6:7], stat[:, 72 + t:73 + t], ALU.subtract, ALU.mult))
                link(v.tensor_tensor(x, x, lngb[:, 0:512], ALU.mult))
                v.tensor_tensor(x, x, lngb[:, 512:1024], ALU.add).then_inc(S("ln_rows"), 1)

            def score_rows(n):
                tile = 1 - n % 2
                w = NG * (T if tile else P)
                mo = 0 if tile else NG * T
                c = 100 + 4 * (n % 2)
                dve.wait_ge(S("scores"), n + 1)
                for lo in range(0, w, 512):
                    m = min(512, w - lo)
                    last = v.tensor_tensor(sc[n % 2][:, lo:lo + m], bank[4 + 2 * (n % 2) + lo // 512][:, 0:m],
                                           amask[:, mo + lo:mo + lo + m], ALU.add)
                link(last)
                link(v.tensor_reduce(stat[:, c + 2:c + 3], sc[n % 2][:, 0:w], AX_X, ALU.max))
                v.tensor_scalar(stat[:, c:c + 1], stat[:, c + 2:c + 3], -(HD ** -0.5), None, ALU.mult) \
                    .then_inc(S("scored"), 1)

            def scale_probs(n):
                w = NG * (P if n % 2 else T)
                c = 100 + 4 * (n % 2)
                dve.wait_ge(S("probs"), n + 1)
                link(v.reciprocal(stat[:, c + 3:c + 4], stat[:, c + 1:c + 2]))
                v.tensor_scalar(sc[n % 2][:, 0:w], sc[n % 2][:, 0:w], stat[:, c + 3:c + 4], None, ALU.mult) \
                    .then_inc(S("probs_scaled"), 1)

            score_rows(0)
            scale_probs(0)
            for n in range(2 * AH):
                tile = 1 - n % 2
                dve.wait_ge(S("probs_turned"), n + 1)
                if tile:
                    dve.wait_ge(S("PT_half"), n // 2 + 1)
                    v.tensor_copy(PTb[:, 512:768], bank[3][:, 0:256]).then_inc(S("PT_ready"), 1)
                if n + 1 < 2 * AH:
                    score_rows(n + 1)
                    scale_probs(n + 1)
                if n == 1:
                    gate_stats()
                if n in (3, 5):
                    gate_rows((n - 3) // 2)
            for t in range(NT):
                dve.wait_ge(S("mixed"), 2)
                x = uv[:, t, 512:1024].rearrange("p (g c) -> p g c", g=SG)
                link(v.tensor_tensor(x, bank[4 + t][:, :].rearrange("p (g c) -> p g c", g=SG),
                                     V("b_spatial_2", 0, 8).unsqueeze(2).to_broadcast([P, SG, HD]), ALU.add))
                v.tensor_tensor(uv[:, t, 0:512], uv[:, t, 0:512], uv[:, t, 512:1024], ALU.mult).then_inc(S("sgu_rows"), 1)
            for t in range(NT):
                dve.wait_ge(S("sgu_turned"), t + 1)
                v.tensor_copy(sT[:, :, t * P:(t + 1) * P], bank[6 + t][:, :].rearrange("p (c t) -> p c t", c=4)) \
                    .then_inc(S("sT_ready"), 1)
            dve.wait_ge(S("gates_sigmoid"), 2)
            merge("proj_a", "proj_b", "merged2", gate[:, 0:KC, :], gate[:, KC:2 * KC, :], mT2, scw)
            add_and_norm("out_merged2", "x3_added", "n4", xn2, 64, None, hn2, "norm2_g_2")
            for c in range(FC):
                dve.wait_ge(S("ff_silu"), c + 1)
                v.tensor_tensor(ffT[:, c, :], sgf[:, c % 4, :], bank[4 + c % 4][:, T:2 * T], ALU.mult) \
                    .then_inc(S("ff_cols"), 1)
            dve.wait_ge(S("fg2_loaded"), 16)
            for t in range(NT):
                add_rows(t, "out_ff_cols", "x4_added")
                dve.wait_ge(S("norm_rstd"), STATS["f2"] + t + 1)
                v.scalar_tensor_tensor(out=outr[:, t, :], in0=h[:, t, :], scalar=stat[:, 104 + t:105 + t], in1=fgb2,
                                       op0=ALU.mult, op1=ALU.mult).then_inc(S("out_rows"), 1)


_INS = ["x", "meta_tokens", "norm1_g", "w_in", "hg_lower_bounds", "hg_norm_g", "conv_w", "conv_b", "lru_w_r",
        "lru_b_r", "lru_w_i", "lru_b_i", "lru_lambda", "w_up_a", "w_up_b", "w_out", "norm2_g", "w_group",
        "b_group", "w_router", "b_router", "w_gate", "w_up", "w_down", "final_g", "positions_2", "norm1_g_2",
        "w_in_2", "sgu_ln_g_2", "sgu_ln_b_2", "w_spatial_2", "b_spatial_2", "w_proj_attn_2", "w_proj_sgu_2",
        "w_out_2", "norm2_g_2", "w_ffn_gate_2", "w_ffn_up_2", "w_ffn_down_2", "final_g_2"]


def kernel(**inputs):
    import numpy as _np
    import concourse.bacc as _bacc
    from concourse import mybir as _mybir
    from concourse.bass_utils import run_bass_kernel_spmd as _run

    nc = _bacc.Bacc("TRN2", target_bir_lowering=False, num_devices=1)
    arrays, aps = {}, {}
    for name in _INS:
        a = _np.ascontiguousarray(inputs[name])
        arrays[f"in_{name}"] = a
        aps[name] = nc.dram_tensor(f"in_{name}", a.shape, _mybir.dt.from_np(a.dtype), kind="ExternalInput").ap()
    out = nc.dram_tensor("out_0", (1, T, D), _mybir.dt.float32, kind="ExternalOutput").ap()
    build(nc, aps, out)
    r = _run(nc, [arrays], core_ids=[0])
    return r.results[0]["out_0"]
```
